# Optimizing a Trainium2 kernel written in Bass

```python
import math
import jax, jax.numpy as jnp
from jax import lax
import numpy as np

D_MODEL = 1024
BATCH = 1
SEQ = 512
DEPTH = 1

ATTN_HEADS = 8
HEAD_DIM = 64
ATTN_WIDTH = ATTN_HEADS * HEAD_DIM
CONV_GROUPS = 8
CONV_CH = D_MODEL - ATTN_WIDTH
MIX_WIDTH = ATTN_WIDTH + CONV_CH
IN_COLS = 3 * ATTN_WIDTH + 2 * CONV_CH
CONV_KERNEL = 31
MOBA_BLOCK = 256
MOBA_TOPK = 3
Q_CHUNK = 128
NUM_BUCKETS = 32
MAX_DISTANCE = 128
D_FF = -(-8 * D_MODEL // (3 * 256)) * 256
RMS_EPS = 1e-6
LN_EPS = 1e-5
NEG_INF = -1e30
ATTN_SCALE = HEAD_DIM ** -0.5


def rms_norm(x, g):
    xf = x.astype(jnp.float32)
    y = xf * lax.rsqrt(jnp.mean(xf * xf, axis=-1, keepdims=True) + RMS_EPS)
    return (y * g.astype(jnp.float32)).astype(x.dtype)

def t5_bucket(dist):
    max_exact = NUM_BUCKETS // 2
    d = jnp.maximum(dist, 1).astype(jnp.float32)
    large = max_exact + (jnp.log(d / max_exact) / math.log(MAX_DISTANCE / max_exact)
                         * (NUM_BUCKETS - max_exact)).astype(jnp.int32)
    large = jnp.minimum(large, NUM_BUCKETS - 1)
    return jnp.where(dist < max_exact, dist, large)

def moba_attention(q, k, v, rel_bias):
    B, H, S, Dh = q.shape
    nb = -(-S // MOBA_BLOCK)
    s_pad = nb * MOBA_BLOCK
    n_sel = max(1, min(MOBA_TOPK, nb - 1))
    nq = S // Q_CHUNK
    pad = ((0, 0), (0, 0), (0, s_pad - S), (0, 0))
    k_blocks = jnp.pad(k, pad).reshape(B, H, nb, MOBA_BLOCK, Dh)
    v_blocks = jnp.pad(v, pad).reshape(B, H, nb, MOBA_BLOCK, Dh)

    k_mean = jnp.mean(k_blocks.astype(jnp.float32), axis=3)
    gate = jnp.einsum('bhsd,bhnd->bhsn', q.astype(jnp.float32), k_mean)
    q_block = jnp.arange(S, dtype=jnp.int32) // MOBA_BLOCK
    fully_past = jnp.arange(nb, dtype=jnp.int32)[None, :] < q_block[:, None]
    gate = jnp.where(fully_past, gate, NEG_INF)
    _, sel = lax.top_k(gate, n_sel)
    sel = sel.astype(jnp.int32)

    bias_ht = rel_bias.T.astype(jnp.float32)
    head_ix = jnp.arange(H)
    offs = jnp.arange(MOBA_BLOCK, dtype=jnp.int32)
    rank_ix = jnp.arange(n_sel, dtype=jnp.int32)

    q_c = q.reshape(B, H, nq, Q_CHUNK, Dh).transpose(0, 2, 1, 3, 4).reshape(B * nq, H, Q_CHUNK, Dh)
    sel_c = sel.reshape(B, H, nq, Q_CHUNK, n_sel).transpose(0, 2, 1, 3, 4).reshape(B * nq, H, Q_CHUNK, n_sel)
    b_ids = jnp.repeat(jnp.arange(B, dtype=jnp.int32), nq)
    c_ids = jnp.tile(jnp.arange(nq, dtype=jnp.int32), B)

    def chunk(args):
        qc, sc, b, c = args
        kb = k_blocks[b]
        vb = v_blocks[b]
        t = c * Q_CHUNK + jnp.arange(Q_CHUNK, dtype=jnp.int32)
        own = (c * Q_CHUNK) // MOBA_BLOCK
        k_sel = kb[head_ix[:, None, None], sc]
        v_sel = vb[head_ix[:, None, None], sc]
        s_sel = jnp.einsum('hqd,hqnkd->hqnk', qc, k_sel).astype(jnp.float32) * ATTN_SCALE
        dist_sel = t[None, :, None, None] - (sc[..., None] * MOBA_BLOCK + offs)
        s_sel = s_sel + bias_ht[head_ix[:, None, None, None], t5_bucket(jnp.maximum(dist_sel, 0))]
        valid = (rank_ix < own)[None, None, :, None]
        s_sel = jnp.where(valid, s_sel, NEG_INF)
        k_own = kb[:, own]
        v_own = vb[:, own]
        s_own = jnp.einsum('hqd,hkd->hqk', qc, k_own).astype(jnp.float32) * ATTN_SCALE
        dist_own = t[:, None] - (own * MOBA_BLOCK + offs)[None, :]
        s_own = s_own + bias_ht[:, t5_bucket(jnp.maximum(dist_own, 0))]
        s_own = jnp.where((dist_own >= 0)[None], s_own, NEG_INF)
        logits = jnp.concatenate([s_sel.reshape(H, Q_CHUNK, n_sel * MOBA_BLOCK), s_own], axis=-1)
        p = jax.nn.softmax(logits, axis=-1).astype(v.dtype)
        p_sel = p[..., :n_sel * MOBA_BLOCK].reshape(H, Q_CHUNK, n_sel, MOBA_BLOCK)
        p_own = p[..., n_sel * MOBA_BLOCK:]
        return (jnp.einsum('hqnk,hqnkd->hqd', p_sel, v_sel)
                + jnp.einsum('hqk,hkd->hqd', p_own, v_own))

    out = lax.map(chunk, (q_c, sel_c, b_ids, c_ids))
    return out.reshape(B, nq, H, Q_CHUNK, Dh).transpose(0, 1, 3, 2, 4).reshape(B, S, H * Dh)

def conformer_conv(a, g, w_dw, b_dw, ln_g, ln_b):
    C = a.shape[-1]
    u = a * jax.nn.sigmoid(g)
    u = lax.conv_general_dilated(u, w_dw[:, None, :], window_strides=(1,),
                                 padding=((CONV_KERNEL - 1, 0),),
                                 dimension_numbers=('NWC', 'WIO', 'NWC'),
                                 feature_group_count=C) + b_dw
    uf = u.astype(jnp.float32)
    mu = jnp.mean(uf, axis=-1, keepdims=True)
    var = jnp.mean(jnp.square(uf - mu), axis=-1, keepdims=True)
    un = (uf - mu) * lax.rsqrt(var + LN_EPS) * ln_g.astype(jnp.float32) + ln_b.astype(jnp.float32)
    return jax.nn.silu(un).astype(a.dtype)

def first_inputs(seed: int = 0) -> dict:
    key = jax.random.key(seed)
    ks = jax.random.split(key, 16)
    f32 = jnp.float32
    nrm = lambda k, shape, scale: jax.random.normal(k, shape, f32) * scale
    return {
        'x': jax.random.normal(ks[0], (BATCH, SEQ, D_MODEL), f32),
        'mix_norm_g': 1.0 + nrm(ks[1], (DEPTH, D_MODEL), 0.02),
        'w_in': nrm(ks[2], (DEPTH, D_MODEL, IN_COLS), D_MODEL ** -0.5),
        'rel_bias': nrm(ks[3], (NUM_BUCKETS, ATTN_HEADS), 0.5),
        'conv_w': nrm(ks[4], (DEPTH, CONV_KERNEL, CONV_CH), CONV_KERNEL ** -0.5),
        'conv_b': nrm(ks[5], (DEPTH, CONV_CH), 0.02),
        'conv_ln_g': 1.0 + nrm(ks[6], (DEPTH, CONV_CH), 0.02),
        'conv_ln_b': nrm(ks[7], (DEPTH, CONV_CH), 0.02),
        'w_out': nrm(ks[8], (DEPTH, MIX_WIDTH, D_MODEL), MIX_WIDTH ** -0.5),
        'ffn_norm_g': 1.0 + nrm(ks[9], (DEPTH, D_MODEL), 0.02),
        'w_gate': nrm(ks[10], (DEPTH, D_MODEL, D_FF), D_MODEL ** -0.5),
        'w_up': nrm(ks[11], (DEPTH, D_MODEL, D_FF), D_MODEL ** -0.5),
        'w_down': nrm(ks[12], (DEPTH, D_FF, D_MODEL), D_FF ** -0.5),
        'final_norm_g': 1.0 + nrm(ks[13], (D_MODEL,), 0.02),
    }

def first_block(x, mix_norm_g, w_in, rel_bias, conv_w, conv_b, conv_ln_g, conv_ln_b,
              w_out, ffn_norm_g, w_gate, w_up, w_down, final_norm_g):
    B, S, _ = x.shape
    splits = [ATTN_WIDTH, 2 * ATTN_WIDTH, 3 * ATTN_WIDTH, 3 * ATTN_WIDTH + CONV_CH]

    def heads(t):
        return t.reshape(B, S, ATTN_HEADS, HEAD_DIM).transpose(0, 2, 1, 3)

    h = x
    for l in range(DEPTH):
        u = rms_norm(h, mix_norm_g[l])
        proj = u @ w_in[l]
        q, k, v, glu_a, glu_g = jnp.split(proj, splits, axis=-1)
        attn_out = moba_attention(heads(q), heads(k), heads(v), rel_bias)
        conv_out = conformer_conv(glu_a, glu_g, conv_w[l], conv_b[l],
                                  conv_ln_g[l], conv_ln_b[l])
        mixed = jnp.concatenate([attn_out, conv_out], axis=-1)
        h = h + mixed @ w_out[l]
        u = rms_norm(h, ffn_norm_g[l])
        h = h + (jax.nn.silu(u @ w_gate[l]) * (u @ w_up[l])) @ w_down[l]
    return rms_norm(h, final_norm_g)


DEPTH_2 = 2

ROT_DIM = HEAD_DIM // 4
ROPE_THETA = 500000.0
Q_BLOCK = 128
EPS = 1e-6

FOX_HEADS = D_MODEL // (2 * HEAD_DIM)
FOX_WIDTH = FOX_HEADS * HEAD_DIM
FOX_FGATE_BIAS = 3.0
DIFF_V_DIM = 2 * HEAD_DIM
DIFF_HEADS = D_MODEL // (2 * DIFF_V_DIM)
DIFF_WIDTH = DIFF_HEADS * DIFF_V_DIM
DSA_HEADS = D_MODEL // (2 * HEAD_DIM)
DSA_NOPE = HEAD_DIM - ROT_DIM
DSA_WIDTH = DSA_HEADS * HEAD_DIM
DSA_KV_RANK = 128
IDX_HEADS = 4
IDX_DIM = 64
IDX_TOPK_MAX = 256
SB_HEADS = D_MODEL // (2 * HEAD_DIM)
SB_WIDTH = SB_HEADS * HEAD_DIM
D_FF_2 = 2816
CONV_WIDTH = 3

EVEN_SPLITS = (FOX_WIDTH, FOX_WIDTH, FOX_WIDTH, FOX_HEADS,
               DIFF_WIDTH, DIFF_WIDTH, DIFF_WIDTH)
ODD_SPLITS = (DSA_WIDTH, DSA_KV_RANK, ROT_DIM, IDX_HEADS * IDX_DIM, IDX_HEADS, IDX_DIM,
              SB_WIDTH, SB_WIDTH, SB_WIDTH)
EVEN_IN = sum(EVEN_SPLITS)
ODD_IN = sum(ODD_SPLITS)
N_EVEN = (DEPTH_2 + 1) // 2
N_ODD = DEPTH_2 // 2


def rms_norm_2(x, g):
    xf = x.astype(jnp.float32)
    y = xf * lax.rsqrt(jnp.mean(xf * xf, axis=-1, keepdims=True) + EPS)
    return (y * g.astype(jnp.float32)).astype(x.dtype)

def split_cols(z, sizes):
    cuts = []
    acc = 0
    for s in sizes[:-1]:
        acc += s
        cuts.append(acc)
    return jnp.split(z, cuts, axis=-1)

def rope_tables(positions):
    inv_freq = ROPE_THETA ** (-jnp.arange(0, ROT_DIM, 2, dtype=jnp.float32) / ROT_DIM)
    ang = positions.astype(jnp.float32)[..., None] * inv_freq
    return jnp.cos(ang), jnp.sin(ang)

def apply_partial_rope(x, cos, sin):
    half = ROT_DIM // 2
    xr = x[..., :ROT_DIM].astype(jnp.float32)
    x1, x2 = xr[..., :half], xr[..., half:]
    rot = jnp.concatenate([x1 * cos - x2 * sin, x2 * cos + x1 * sin], axis=-1)
    return jnp.concatenate([rot.astype(x.dtype), x[..., ROT_DIM:]], axis=-1)

def sweep(block_fn, seq_len):
    out = lax.map(block_fn, jnp.arange(seq_len // Q_BLOCK))
    out = jnp.moveaxis(out, 0, 1)
    return out.reshape((out.shape[0], seq_len) + out.shape[3:])

def gather_rows(table, idx):
    return jax.vmap(lambda t, i: jnp.take(t, i, axis=0))(table, idx)

def fox_attention(q, k, v, log_f):
    seq_len = q.shape[1]
    scale = HEAD_DIM ** -0.5
    c = jnp.transpose(jnp.cumsum(log_f, axis=1), (0, 2, 1))
    kpos = jnp.arange(seq_len)

    def block(i):
        start = i * Q_BLOCK
        qpos = start + jnp.arange(Q_BLOCK)
        qb = lax.dynamic_slice_in_dim(q, start, Q_BLOCK, axis=1)
        cb = lax.dynamic_slice_in_dim(c, start, Q_BLOCK, axis=2)
        s = jnp.einsum('bqhd,bkhd->bhqk', qb, k).astype(jnp.float32) * scale
        s = s + (cb[..., :, None] - c[..., None, :])
        s = jnp.where(qpos[:, None] >= kpos[None, :], s, -jnp.inf)
        p = jax.nn.softmax(s, axis=-1).astype(v.dtype)
        return jnp.einsum('bhqk,bkhd->bqhd', p, v)

    return sweep(block, seq_len)

def diff_attention(q1, q2, k1, k2, v, lam):
    seq_len = q1.shape[1]
    scale = HEAD_DIM ** -0.5
    kpos = jnp.arange(seq_len)

    def block(i):
        start = i * Q_BLOCK
        qpos = start + jnp.arange(Q_BLOCK)
        mask = qpos[:, None] >= kpos[None, :]
        q1b = lax.dynamic_slice_in_dim(q1, start, Q_BLOCK, axis=1)
        q2b = lax.dynamic_slice_in_dim(q2, start, Q_BLOCK, axis=1)
        s1 = jnp.einsum('bqhd,bkhd->bhqk', q1b, k1).astype(jnp.float32) * scale
        s2 = jnp.einsum('bqhd,bkhd->bhqk', q2b, k2).astype(jnp.float32) * scale
        p1 = jax.nn.softmax(jnp.where(mask, s1, -jnp.inf), axis=-1)
        p2 = jax.nn.softmax(jnp.where(mask, s2, -jnp.inf), axis=-1)
        p = (p1 - lam * p2).astype(v.dtype)
        return jnp.einsum('bhqk,bkhd->bqhd', p, v)

    return sweep(block, seq_len)

def stick_breaking_attention(q, k, v):
    seq_len = q.shape[1]
    scale = HEAD_DIM ** -0.5
    kpos = jnp.arange(seq_len)

    def block(i):
        start = i * Q_BLOCK
        qpos = start + jnp.arange(Q_BLOCK)
        mask = kpos[None, :] < qpos[:, None]
        qb = lax.dynamic_slice_in_dim(q, start, Q_BLOCK, axis=1)
        z = jnp.einsum('bqhd,bkhd->bhqk', qb, k).astype(jnp.float32) * scale
        log1m = jnp.where(mask, jax.nn.log_sigmoid(-z), 0.0)
        after = lax.cumsum(log1m, axis=3, reverse=True) - log1m
        a = jnp.where(mask, jnp.exp(jax.nn.log_sigmoid(z) + after), 0.0)
        return jnp.einsum('bhqk,bkhd->bqhd', a.astype(v.dtype), v)

    return sweep(block, seq_len)

def dsa_attention(q_abs, q_rope, c_kv, k_rope, iq, iw, ik, top_k):
    seq_len = q_abs.shape[1]
    scale = HEAD_DIM ** -0.5
    kpos = jnp.arange(seq_len)

    def block(i):
        start = i * Q_BLOCK
        qpos = start + jnp.arange(Q_BLOCK)
        iqb = lax.dynamic_slice_in_dim(iq, start, Q_BLOCK, axis=1)
        iwb = lax.dynamic_slice_in_dim(iw, start, Q_BLOCK, axis=1)
        logits = jnp.einsum('bqhd,bkd->bqhk', iqb, ik).astype(jnp.float32)
        score = jnp.einsum('bqhk,bqh->bqk', jax.nn.relu(logits), iwb.astype(jnp.float32))
        score = jnp.where(kpos[None, None, :] <= qpos[None, :, None], score, -jnp.inf)
        _, sel = lax.top_k(score, top_k)
        valid = sel <= qpos[None, :, None]
        c_sel = gather_rows(c_kv, sel)
        kr_sel = gather_rows(k_rope, sel)
        qab = lax.dynamic_slice_in_dim(q_abs, start, Q_BLOCK, axis=1)
        qrb = lax.dynamic_slice_in_dim(q_rope, start, Q_BLOCK, axis=1)
        s = (jnp.einsum('bqhr,bqkr->bqhk', qab, c_sel)
             + jnp.einsum('bqhd,bqkd->bqhk', qrb, kr_sel)).astype(jnp.float32) * scale
        s = jnp.where(valid[:, :, None, :], s, -jnp.inf)
        p = jax.nn.softmax(s, axis=-1).astype(c_kv.dtype)
        return jnp.einsum('bqhk,bqkr->bqhr', p, c_sel)

    return sweep(block, seq_len)

def even_mixer(h, cos, sin, w_in, fgate_b, lq1, lk1, lq2, lk2, subln, w_out, layer_idx):
    b, s, _ = h.shape
    aq, ak, av, af, bq, bk, bv = split_cols(h @ w_in, EVEN_SPLITS)
    log_f = jax.nn.log_sigmoid((af + fgate_b).astype(jnp.float32))
    o_a = fox_attention(aq.reshape(b, s, FOX_HEADS, HEAD_DIM),
                        ak.reshape(b, s, FOX_HEADS, HEAD_DIM),
                        av.reshape(b, s, FOX_HEADS, HEAD_DIM), log_f)
    cs, sn = cos[:, :, None, :], sin[:, :, None, :]
    bq = bq.reshape(b, s, DIFF_HEADS, 2, HEAD_DIM)
    bk = bk.reshape(b, s, DIFF_HEADS, 2, HEAD_DIM)
    q1 = apply_partial_rope(bq[..., 0, :], cs, sn)
    q2 = apply_partial_rope(bq[..., 1, :], cs, sn)
    k1 = apply_partial_rope(bk[..., 0, :], cs, sn)
    k2 = apply_partial_rope(bk[..., 1, :], cs, sn)
    lam_init = 0.8 - 0.6 * math.exp(-0.3 * layer_idx)
    lam = (jnp.exp(jnp.sum(lq1.astype(jnp.float32) * lk1.astype(jnp.float32)))
           - jnp.exp(jnp.sum(lq2.astype(jnp.float32) * lk2.astype(jnp.float32))) + lam_init)
    o_b = diff_attention(q1, q2, k1, k2, bv.reshape(b, s, DIFF_HEADS, DIFF_V_DIM), lam)
    o_b = rms_norm_2(o_b, subln) * (1.0 - lam_init)
    o = jnp.concatenate([o_a.reshape(b, s, FOX_WIDTH), o_b.reshape(b, s, DIFF_WIDTH)], axis=-1)
    return o @ w_out

def odd_mixer(h, cos, sin, w_in, kv_norm, w_uk, w_uv, w_out, top_k):
    b, s, _ = h.shape
    cq, ckv, ckr, ciq, ciw, cik, sq, sk, sv = split_cols(h @ w_in, ODD_SPLITS)
    cs, sn = cos[:, :, None, :], sin[:, :, None, :]
    cq = apply_partial_rope(cq.reshape(b, s, DSA_HEADS, HEAD_DIM), cs, sn)
    q_rope, q_nope = cq[..., :ROT_DIM], cq[..., ROT_DIM:]
    c_kv = rms_norm_2(ckv, kv_norm)
    k_rope = apply_partial_rope(ckr, cos, sin)
    q_abs = jnp.einsum('bshn,rhn->bshr', q_nope, w_uk)
    iq = apply_partial_rope(ciq.reshape(b, s, IDX_HEADS, IDX_DIM), cs, sn)
    ik = apply_partial_rope(cik, cos, sin)
    iw = ciw * (IDX_HEADS ** -0.5)
    o_lat = dsa_attention(q_abs, q_rope, c_kv, k_rope, iq, iw, ik, top_k)
    o_c = jnp.einsum('bshr,rhd->bshd', o_lat, w_uv).reshape(b, s, DSA_WIDTH)
    o_d = stick_breaking_attention(sq.reshape(b, s, SB_HEADS, HEAD_DIM),
                                   sk.reshape(b, s, SB_HEADS, HEAD_DIM),
                                   sv.reshape(b, s, SB_HEADS, HEAD_DIM)).reshape(b, s, SB_WIDTH)
    return jnp.concatenate([o_c, o_d], axis=-1) @ w_out

def conv_ffn(h, w_in, conv_w, conv_b, w_out):
    u = h @ w_in
    u = lax.conv_general_dilated(u, conv_w[:, None, :], window_strides=(1,),
                                 padding=[(CONV_WIDTH - 1, 0)],
                                 dimension_numbers=('NWC', 'WIO', 'NWC'),
                                 feature_group_count=u.shape[-1]) + conv_b
    g, v = jnp.split(u, 2, axis=-1)
    return (jax.nn.silu(g) * v) @ w_out

def second_inputs(seed: int = 0) -> dict:
    key = jax.random.key(seed)
    ks = jax.random.split(key, 24)
    f32 = jnp.float32

    def nrm(k, shape, scale):
        return jax.random.normal(k, shape, f32) * scale

    return {
        "x": nrm(ks[0], (BATCH, SEQ, D_MODEL), 1.0),
        "positions": jnp.broadcast_to(jnp.arange(SEQ, dtype=jnp.int32), (BATCH, SEQ)),
        "attn_norm": 1.0 + nrm(ks[1], (DEPTH_2, D_MODEL), 0.02),
        "ffn_norm": 1.0 + nrm(ks[2], (DEPTH_2, D_MODEL), 0.02),
        "final_norm": 1.0 + nrm(ks[3], (D_MODEL,), 0.02),
        "ev_w_in": nrm(ks[4], (N_EVEN, D_MODEL, EVEN_IN), D_MODEL ** -0.5),
        "ev_fgate_b": FOX_FGATE_BIAS + nrm(ks[5], (N_EVEN, FOX_HEADS), 0.1),
        "ev_lambda_q1": nrm(ks[6], (N_EVEN, HEAD_DIM), 0.1),
        "ev_lambda_k1": nrm(ks[7], (N_EVEN, HEAD_DIM), 0.1),
        "ev_lambda_q2": nrm(ks[8], (N_EVEN, HEAD_DIM), 0.1),
        "ev_lambda_k2": nrm(ks[9], (N_EVEN, HEAD_DIM), 0.1),
        "ev_subln": 1.0 + nrm(ks[10], (N_EVEN, DIFF_V_DIM), 0.02),
        "ev_w_out": nrm(ks[11], (N_EVEN, D_MODEL, D_MODEL), D_MODEL ** -0.5),
        "od_w_in": nrm(ks[12], (N_ODD, D_MODEL, ODD_IN), D_MODEL ** -0.5),
        "od_kv_norm": 1.0 + nrm(ks[13], (N_ODD, DSA_KV_RANK), 0.02),
        "od_w_uk": nrm(ks[14], (N_ODD, DSA_KV_RANK, DSA_HEADS, DSA_NOPE), DSA_KV_RANK ** -0.5),
        "od_w_uv": nrm(ks[15], (N_ODD, DSA_KV_RANK, DSA_HEADS, HEAD_DIM), DSA_KV_RANK ** -0.5),
        "od_w_out": nrm(ks[16], (N_ODD, D_MODEL, D_MODEL), D_MODEL ** -0.5),
        "ffn_w_in": nrm(ks[17], (DEPTH_2, D_MODEL, 2 * D_FF_2), D_MODEL ** -0.5),
        "ffn_conv_w": nrm(ks[18], (DEPTH_2, CONV_WIDTH, 2 * D_FF_2), CONV_WIDTH ** -0.5),
        "ffn_conv_b": nrm(ks[19], (DEPTH_2, 2 * D_FF_2), 0.02),
        "ffn_w_out": nrm(ks[20], (DEPTH_2, D_FF_2, D_MODEL), D_FF_2 ** -0.5),
    }

def second_block(x, positions, attn_norm, ffn_norm, final_norm,
              ev_w_in, ev_fgate_b, ev_lambda_q1, ev_lambda_k1, ev_lambda_q2, ev_lambda_k2,
              ev_subln, ev_w_out,
              od_w_in, od_kv_norm, od_w_uk, od_w_uv, od_w_out,
              ffn_w_in, ffn_conv_w, ffn_conv_b, ffn_w_out):
    cos, sin = rope_tables(positions)
    top_k = min(IDX_TOPK_MAX, x.shape[1] // 4)
    for layer in range(DEPTH_2):
        j = layer // 2
        h = rms_norm_2(x, attn_norm[layer])
        if layer % 2 == 0:
            x = x + even_mixer(h, cos, sin, ev_w_in[j], ev_fgate_b[j],
                               ev_lambda_q1[j], ev_lambda_k1[j], ev_lambda_q2[j], ev_lambda_k2[j],
                               ev_subln[j], ev_w_out[j], layer)
        else:
            x = x + odd_mixer(h, cos, sin, od_w_in[j], od_kv_norm[j], od_w_uk[j], od_w_uv[j],
                              od_w_out[j], top_k)
        h = rms_norm_2(x, ffn_norm[layer])
        x = x + conv_ffn(h, ffn_w_in[layer], ffn_conv_w[layer], ffn_conv_b[layer], ffn_w_out[layer])
    return rms_norm_2(x, final_norm)


def setup_inputs(seed=0):
    out = dict(first_inputs(seed))
    for name, value in second_inputs(seed + 1).items():
        if name != "x":
            out[name + "_2"] = value
    return out


def reference(
    x, mix_norm_g, w_in, rel_bias, conv_w, conv_b, conv_ln_g, conv_ln_b, w_out, ffn_norm_g,
    w_gate, w_up, w_down, final_norm_g, positions_2, attn_norm_2, ffn_norm_2, final_norm_2,
    ev_w_in_2, ev_fgate_b_2, ev_lambda_q1_2, ev_lambda_k1_2, ev_lambda_q2_2, ev_lambda_k2_2,
    ev_subln_2, ev_w_out_2, od_w_in_2, od_kv_norm_2, od_w_uk_2, od_w_uv_2, od_w_out_2,
    ffn_w_in_2, ffn_conv_w_2, ffn_conv_b_2, ffn_w_out_2,
):
    x = first_block(
        x, mix_norm_g, w_in, rel_bias, conv_w, conv_b, conv_ln_g, conv_ln_b, w_out, ffn_norm_g,
        w_gate, w_up, w_down, final_norm_g,
    )
    return second_block(
        x, positions_2, attn_norm_2, ffn_norm_2, final_norm_2, ev_w_in_2, ev_fgate_b_2,
        ev_lambda_q1_2, ev_lambda_k1_2, ev_lambda_q2_2, ev_lambda_k2_2, ev_subln_2, ev_w_out_2,
        od_w_in_2, od_kv_norm_2, od_w_uk_2, od_w_uv_2, od_w_out_2, ffn_w_in_2, ffn_conv_w_2,
        ffn_conv_b_2, ffn_w_out_2,
    )


_drawn_inputs = setup_inputs


def setup_inputs(seed=0):
    import zlib

    import numpy as np

    out = dict(_drawn_inputs(seed))
    spreads = {}
    factors = {'mix_norm_g': 3.44,
     'conv_ln_g': 2.782,
     'ffn_norm_g': 3.068,
     'ffn_norm_2': 2.965,
     'final_norm_2': 8.077,
     'ev_fgate_b_2': 26.624,
     'ev_subln_2': 4.281,
     'od_kv_norm_2': 8.0,
     'ffn_conv_b_2': 2.908}
    for name, (base, spread) in spreads.items():
        noise = np.random.default_rng([zlib.crc32(name.encode()), seed]).standard_normal(out[name].shape)
        drawn = base * np.exp(spread * noise) if base else spread * noise
        out[name] = __import__('jax').numpy.asarray(drawn.astype(out[name].dtype))
    for name, factor in factors.items():
        out[name] = (out[name] * factor).astype(out[name].dtype)
    return out
```

```python
from contextlib import ExitStack
import math

import numpy as np

import concourse.bass as bass
from concourse import mybir

F32 = mybir.dt.float32
F32R = mybir.dt.float32r
BF16 = mybir.dt.bfloat16
I32 = mybir.dt.int32
ALU = mybir.AluOpType
ACT = mybir.ActivationFunctionType
AX = mybir.AxisListType

P = 128
S = 512
D = 1024
DC = D // P
HD = 64
HEADS = 8
FF = 2816
FC = FF // P
QT = S // P
TAPS = 31
PADL = TAPS - 1
RANK = 128
IDXH = 4
TOPK = min(256, S // 4)
DIFFH = 4
SCALE = HD ** -0.5
NEG = -1e30
TAKEN = -3e38
EPS = 1e-6
LN_EPS = 1e-5
LAM_INIT = 0.8 - 0.6 * math.exp(-0.3 * 0)
MAGIC = 12582912.0
TWO_PI = (6.28125, 0.0019350051879882812, 3.019915981956753e-07)

PHASES = [("in1", 10), ("out1", 4), ("up1", FC), ("down1", 12),
          ("in2", 13), ("out2", 4), ("up2", FC), ("down2", 12),
          ("in3", 11), ("out3", 4), ("up3", FC), ("down3", 12)]
BASE, PAIR = {}, {}
_n = _o = 0
for _name, _k in PHASES:
    BASE[_name], PAIR[_name] = _n, _o
    _n += _k
    _o += 4 if _name.startswith("down") else _k
NSLAB = _n
DOWN_K = (8, 8, 6)

COL = {}
_c = 0
for _name, _k in [("gain", 8 * DC), ("conv_w", 4 * TAPS), ("conv_b", 4), ("ln_g", 4), ("ln_b", 4),
                  ("ffn2", FC * 8), ("ffn3", FC * 8), ("subln", 1), ("kv_norm", 1), ("fgate_b", 1),
                  ("lam", 4), ("freq", 1), ("rope_rows", 1), ("half_pi", 1), ("eps", 1), ("ln_eps", 1),
                  ("one", 1)]:
    COL[_name] = _c
    _c += _k
NCOL = _c


FILLS = [("norm0", 8, 8), ("att1", 8, 4), ("norm1", 8, 8), ("norm3", 8, 8), ("att2", 8, 4),
         ("norm4", 8, 8), ("norm5", 8, 8), ("att3", 12, 0), ("norm6", 8, 8)]
FILL, LOWS = {}, {}
_f = _l = 0
for _name, _h, _k in FILLS:
    FILL[_name], LOWS[_name] = _f, _l
    _f += _h
    _l += _k

UPDATE = {"out1": 0, "down1": 1, "norm2": 2, "out2": 3, "down2": 4, "out3": 5, "down3": 6, "norm7": 7}
QKV = {"in1": 0, "in2": 6, "in3": 19}


def bank_free():
    free = {}
    for name, k in PHASES:
        for j in range(4 if name.startswith("down") else k):
            o = PAIR[name] + j
            if name in ("out1", "out2", "out3", "down1", "down2", "down3"):
                free[o] = ("x", DC * UPDATE[name] + 2 * j + 2)
            elif name == "in1":
                free[o] = ("glu", j + 1) if j < 4 else ("qkv", j - 3)
            elif name in ("in2", "in3"):
                free[o] = ("qkv", QKV[name] + j + 1)
            elif name == "up1":
                free[o] = ("h", j + 1)
            else:
                free[o] = ("fconv", (FC if name == "up3" else 0) + j + 1)
    return free


BANK_FREE = bank_free()


class Unit:
    pass


def plan_units():
    units, n_set, n_bs, n_mx, n_pr, n_sb, group = {1: [], 2: [], 3: []}, 0, 0, 0, 0, 0, 0
    total = 0
    for t, kind, heads in ((1, "moba", 8), (2, "fox", 8), (2, "diff", DIFFH), (3, "sb", 8), (3, "dsa", 8)):
        for h in range(heads):
            for qt in range(QT):
                u = Unit()
                u.t, u.kind, u.h, u.qt, u.w, u.n = t, kind, h, qt, P * (qt + 1), total
                u.half = HD * (h % 2)
                u.sets = [n_set, n_set + 1] if kind == "diff" else [n_set]
                n_set += len(u.sets)
                n_bs += kind in ("moba", "fox")
                n_mx += 0 if kind == "sb" else len(u.sets)
                n_pr += kind != "sb"
                n_sb += kind == "sb"
                u.bs, u.mx, u.pr, u.sb = n_bs, n_mx, n_pr, n_sb
                paired = kind in ("moba", "fox", "sb")
                u.group = group
                u.first = qt == 0 and not (paired and h % 2)
                u.last = qt == QT - 1 and (h % 2 == 1 or not paired)
                group += u.last
                units[t].append(u)
                total += 1
    return units


UNITS = plan_units()
DSA_GROUP0 = UNITS[3][32].group
DIFF_GROUP0 = UNITS[2][32].group
AHEAD = {"moba": 2, "fox": 2, "diff": 1, "sb": 2, "dsa": 2}


def runs_of(t):
    out = []
    for u in UNITS[t]:
        if not out or out[-1][0].kind != u.kind:
            out.append([])
        out[-1].append(u)
    return out


SEMS = (
    "consts", "x_in", "bias_in", "rows_out", "bias_out",
    "whi", "wlo", "slab",
    "sq", "sums", "root", "rstd", "u",
    "ahi", "alo", "x",
    "lin", "fconv", "fstep", "silu", "h", "hhi", "hlo",
    "pad", "glu_g", "glu", "taps", "ln_sum", "ln_act", "ln_dve", "brow_mm", "brow_ev", "masks",
    "rope_dve", "rope_act",
    "qkv", "rot", "rope_t", "rope_c", "rope", "fg_act", "fg_dve", "cq_mm", "cq_ev", "nc_mm", "nc_ev",
    "lam_dve", "lam_mm", "lam_act",
    "sel_in", "l3_in", "kv_sq", "kv_sum", "kv_root", "kv_dve", "kv_tr", "kv_ev", "iw_tr", "iw_ev",
    "lg_mm", "lg_relu", "score", "top8", "topr", "selm", "qa_mm", "qa_ev", "ol_ev", "uv_mm",
    "sc", "bs", "mx", "ex", "fac", "pr", "tr", "pt", "pv", "sb_act", "sb_dve",
    "df_sq", "df_sum", "df_root", "df_rec", "df_out", "oev",
)


def build(nc, weights, vectors, x_in, positions, bias_rows, buckets, selectors, uk, uv,
          squares, out):
    ctx = ExitStack()
    rows_dram = nc.dram_tensor("bias_rows_scratch", (HEADS, P, 640), F32, kind="Internal").ap()
    with ctx:
        def sb(name, shape, dt=F32):
            return ctx.enter_context(nc.sbuf_tensor(name, shape, dt))

        xT = sb("xT", [P, DC, S])
        a_hi = sb("a_hi", [P, DC, S], F32R)
        a_lo = sb("a_lo", [P, DC, S], F32R)
        raw = sb("raw", [P, 2, 2048])
        w_hi = sb("w_hi", [P, 2, 2048], F32R)
        w_lo = sb("w_lo", [P, 2, 2048], F32R)
        tmp = sb("tmp", [P, 6, S])
        cosT = sb("cosT", [P, S])
        sinT = sb("sinT", [P, S])
        vec = sb("vec", [P, NCOL])
        sq_f = sb("sq_f", [P, 3, P])
        sq_b = sb("sq_b", [P, 3, P], BF16)
        small = sb("small", [P, 16])
        stat = sb("stat", [P, 4, 4])
        ones, ident, rotm = sq_f[:, 0, :], sq_f[:, 1, :], sq_f[:, 2, :]
        ident_b, tri_b, strict_b = sq_b[:, 0, :], sq_b[:, 1, :], sq_b[:, 2, :]

        def col(name, i=0):
            return vec[:, COL[name] + i:COL[name] + i + 1]

        def area(*wanted):
            with ExitStack() as here:
                return [here.enter_context(nc.sbuf_tensor(n, s, d)) for n, s, d in wanted]

        h_hi, h_lo = area(("h_hi", [P, FC, S], F32R), ("h_lo", [P, FC, S], F32R))
        common = [("e", [P, 4, S], F32), ("pT", [P, 2, S], F32), ("sbi", [P, 3, S], F32)]
        e1_, pT1, sbi1, qk1, v1, bias_t, cu, cacc, brow, bb, oh = area(
            *[(n + "1", s, d) for n, s, d in common],
            ("qk1", [P, 8, S], F32), ("v1", [P, QT, 512], F32), ("bias_t", [P, HEADS, S], F32),
            ("cu", [P, 4, PADL + S], F32), ("cacc", [P, 4, S], F32), ("brow", [HEADS, 640], F32),
            ("bb", [33, HEADS], F32), ("oh", [33, 640], F32))
        e2_, pT2, sbi2, qk2, v2, ncb, fg, cq_t, sel8 = area(
            *[(n + "2", s, d) for n, s, d in common],
            ("qk2", [P, 16, S], F32), ("v2", [P, QT, 1024], F32), ("ncb", [P, 2, S], F32),
            ("fg", [HEADS, 3, S], F32), ("cq_t", [P, QT, HEADS], F32), ("sel8", [HEADS, HEADS * P], F32))
        e3_, pT3, sbi3, qk3, v3, ckv, ckv_t, qabs, olat, wuk, wuv, iwq, score, selm, max8 = area(
            *[(n + "3", s, d) for n, s, d in common],
            ("qk3", [P, 16, S], F32), ("v3", [P, QT, 512], F32), ("ckv", [P, S], F32),
            ("ckv_t", [P, QT, RANK], F32), ("qabs", [P, 2, S], F32), ("olat", [P, 2, S], F32),
            ("wuk", [P, 4, RANK], F32), ("wuv", [P, 512], F32), ("iwq", [P, QT, IDXH], F32),
            ("score", [P, 3, S], F32), ("selm", [P, 4, S], BF16), ("max8", [P, 3, 8], F32))
        E = {1: e1_, 2: e2_, 3: e3_}
        PT = {1: pT1, 2: pT2, 3: pT3}
        SBI = {1: sbi1, 2: sbi2, 3: sbi3}
        QK = {1: qk1, 2: qk2, 3: qk3}
        V = {1: v1, 2: v2, 3: v3}

        ps = ctx.enter_context(nc.psum_tensor("ps", [P, 8, 512], F32))
        BX, BT, BO = 3, 4, 6

        sem = {name: ctx.enter_context(nc.semaphore("s_" + name)) for name in SEMS}
        landed = [ctx.enter_context(nc.semaphore(f"s_landed{j}")) for j in range(2)]
        s_out = ctx.enter_context(nc.semaphore("s_out"))
        block = ctx.enter_context(nc.Block())

        def ready_x(k, c):
            return DC * (k - 1) + c + 1

        @block.sync
        def _(sp):
            for n in range(2):
                sp.dma_start(raw[:, n, :], weights[n]).then_inc(landed[n], 16)
            with sp.Fori(0, NSLAB // 2 - 1) as i:
                for j in range(2):
                    sp.wait_ge(sem["wlo"], i * 2 + (j + 1))
                    sp.dma_start(raw[:, j, :], weights[i * 2 + (j + 2)]).then_inc(landed[j], 16)
            for c in range(DC):
                sp.wait_ge(sem["x"], DC * UPDATE["norm7"] + c + 1)
                sp.dma_start(out[c], xT[:, c, :]).then_inc(s_out, 16)
            sp.wait_ge(s_out, 16 * DC)

        @block.gpsimd
        def _(pool):
            for c in range(DC):
                pool.dma_start(xT[:, c, :], x_in[c]).then_inc(sem["x_in"], 16)
            pool.dma_start(vec[:, :], vectors).then_inc(sem["consts"], 16)
            pool.dma_start(sq_f[:, :, :], squares[:, 0:3, :]).then_inc(sem["consts"], 16)
            pool.dma_start(tmp[:, 5, 0:2 * P].rearrange("p (a b) -> p a b", a=2),
                           squares[:, 3:5, :]).then_inc(sem["consts"], 16)
            pool.dma_start(tmp[:, 4, :].bitcast(I32), positions.to_broadcast([P, S])).then_inc(sem["consts"], 16)
            pool.dma_start(bb[:, :], bias_rows).then_inc(sem["bias_in"], 16)
            pool.dma_start(oh[:, :], buckets).then_inc(sem["bias_in"], 16)
            pool.wait_ge(sem["brow_ev"], 2)
            for h in range(HEADS):
                pool.dma_start(rows_dram[h:h + 1], brow[h:h + 1, :].unsqueeze(1).to_broadcast([1, P, 640])
                               ).then_inc(sem["rows_out"], 16)
            pool.wait_ge(sem["rows_out"], 16 * HEADS)
            for h in range(HEADS):
                shifted = bass.AP(tensor=rows_dram.tensor, offset=h * P * 640 + P - 1,
                                  ap=[[639, P], [1, S]])
                pool.dma_start(bias_t[:, h, :], shifted).then_inc(sem["bias_out"], 16)
            pool.wait_ge(sem["slab"], BASE["in2"])
            pool.dma_start(sel8[:, :], selectors).then_inc(sem["sel_in"], 16)
            pool.wait_ge(sem["slab"], BASE["in3"])
            pool.dma_start(wuk[:, :, :], uk).then_inc(sem["l3_in"], 16)
            pool.dma_start(wuv[:, :], uv).then_inc(sem["l3_in"], 16)

        @block.tensor
        def _(pe):
            def wait(name, value):
                pe.wait_ge(sem[name], value)

            def slab_waits(n, o):
                wait("wlo", n + 1)
                if o >= 2:
                    wait(*BANK_FREE[o - 2])

            def feature_major(slot, bank, hi, lo, k0, nk, start, stop, fill=None, halves=(0, 1)):
                for k in range(nk):
                    if fill is not None:
                        fill(k0 + k)
                    for half in halves:
                        c = k * 256 + half * P
                        wh, wl = w_hi[:, slot, c:c + P], w_lo[:, slot, c:c + P]
                        dst = ps[:, bank + half, :]
                        pe.matmul(dst, wh, hi[:, k0 + k, :], start=start and k == 0, stop=False)
                        pe.matmul(dst, wh, lo[:, k0 + k, :], start=False, stop=False)
                        last = pe.matmul(dst, wl, hi[:, k0 + k, :], start=False,
                                         stop=stop and k == nk - 1)
                return last

            def token_major(slot, bank):
                for t in range(QT):
                    dst = ps[:, bank + t // 2, (t % 2) * 256:(t % 2) * 256 + 256]
                    for k in range(DC):
                        c = k * 256
                        ah, al = a_hi[:, k, t * P:(t + 1) * P], a_lo[:, k, t * P:(t + 1) * P]
                        pe.matmul(dst, ah, w_hi[:, slot, c:c + 256], start=k == 0, stop=False)
                        pe.matmul(dst, ah, w_lo[:, slot, c:c + 256], start=False, stop=False)
                        last = pe.matmul(dst, al, w_hi[:, slot, c:c + 256], start=False, stop=k == DC - 1)
                return last

            def in_fill(name):
                return lambda k: wait("alo", LOWS[name] + k + 1)

            def project(name, j, fill=None, halves=(0, 1), tokens=False):
                n, o = BASE[name] + j, PAIR[name] + j
                slab_waits(n, o)
                bank = 2 * (o % 2)
                if tokens:
                    last = token_major(n % 2, bank)
                else:
                    last = feature_major(n % 2, bank, a_hi, a_lo, 0, DC, True, True, fill, halves)
                last.then_inc(sem["slab"], 1)

            def norm_sum(k, c):
                wait("sq", DC * k + c + 1)
                pe.matmul(ps[:, BT, :], ones, tmp[:, c % 2, :], start=c == 0,
                          stop=c == DC - 1).then_inc(sem["sums"], 1)

            def out_proj(name, fill, k):
                wait("oev", UNITS[int(fill[-1])][-1].group + 1)
                wait("alo", LOWS[fill] + (4 if fill != "att3" else 0))
                for j in range(4):
                    project(name, j)
                    if j:
                        norm_sum(k, 2 * j - 2)
                        norm_sum(k, 2 * j - 1)
                norm_sum(k, 6)
                norm_sum(k, 7)

            def ffn_up(name, norm):
                for j in range(2):
                    project(name, j, in_fill(norm) if j == 0 else None)
                free, value = BANK_FREE[PAIR[name]]
                with pe.Fori(0, FC // 2 - 1) as i:
                    for j in range(2):
                        n = BASE[name] + 2 + j
                        o = PAIR[name] + 2 + j
                        pe.wait_ge(sem["wlo"], i * 2 + (n + 1))
                        pe.wait_ge(sem[free], i * 2 + (value + j))
                        feature_major(n % 2, 2 * (o % 2), a_hi, a_lo, 0, DC, True, True
                                      ).then_inc(sem["slab"], 1)

            def ffn_down(name, f, k):
                for p in range(4):
                    k0 = 0
                    for t, nk in enumerate(DOWN_K):
                        n = BASE[name] + 3 * p + t
                        o = PAIR[name] + p
                        wait("wlo", n + 1)
                        if t == 0:
                            wait(*BANK_FREE[o - 2])
                        fill = (lambda c: wait("hlo", FC * f + c + 1)) if p == 0 else None
                        feature_major(n % 2, 2 * (o % 2), h_hi, h_lo, k0, nk, t == 0, t == 2,
                                      fill).then_inc(sem["slab"], 1)
                        k0 += nk
                    if p:
                        norm_sum(k, 2 * p - 2)
                        norm_sum(k, 2 * p - 1)
                norm_sum(k, 6)
                norm_sum(k, 7)

            def rotate(t, r, chunk):
                if r >= 2:
                    wait("rope_t", r - 1)
                pe.matmul(ps[:, BT + r % 2, :], rotm, QK[t][:, chunk, :], start=True,
                          stop=True).then_inc(sem["rot"], 1)

            def scores(u):
                q = slice(u.qt * P, (u.qt + 1) * P)
                for j, st in enumerate(u.sets):
                    if st >= 3:
                        wait("ex", st - 2)
                    dst = ps[:, st % 3, 0:u.w]
                    diag = ps[:, st % 3, u.w - P:u.w]
                    f = slice(u.half, u.half + HD)
                    if u.kind == "moba":
                        m = pe.matmul(dst, qk1[f, u.h // 2, q], qk1[f, 4 + u.h // 2, 0:u.w],
                                      start=True, stop=True)
                    elif u.kind == "dsa":
                        wait("qa_ev", u.h + 1)
                        pe.matmul(dst, qabs[:, u.h % 2, q], ckv[:, 0:u.w], start=True, stop=False)
                        pe.matmul(dst, qk3[f, 4 + u.h // 2, q], qk3[f, 0, 0:u.w], start=False, stop=False)
                        m = pe.matmul(dst, ident_b, selm[:, u.qt, 0:u.w], start=False, stop=True)
                    else:
                        if u.kind == "fox":
                            qq, kk, mask = qk2[f, u.h // 2, q], qk2[f, 4 + u.h // 2, 0:u.w], tri_b
                        elif u.kind == "diff":
                            f = slice(HD * j, HD * j + HD)
                            qq, kk, mask = qk2[f, 8 + u.h, q], qk2[f, 12 + u.h, 0:u.w], tri_b
                        else:
                            qq, kk, mask = qk3[f, 8 + u.h // 2, q], qk3[f, 12 + u.h // 2, 0:u.w], strict_b
                        pe.matmul(dst, qq, kk, start=True, stop=False)
                        m = pe.matmul(diag, ident_b, mask, start=False, stop=True)
                    m.then_inc(sem["sc"], 1)

            def turn(u):
                if u.kind == "sb":
                    wait("ex", u.sets[0] + 1)
                else:
                    wait("pr", u.pr)
                if u.n >= 2:
                    wait("pt", u.n - 1)
                e = E[u.t][:, u.sets[0] % 4, :]
                for b in range(u.qt + 1):
                    m = pe.transpose(ps[:, BT + u.n % 2, b * P:(b + 1) * P], e[:, b * P:(b + 1) * P], ident)
                m.then_inc(sem["tr"], 1)

            def values(u):
                wait("pt", u.n + 1)
                if u.first and u.group >= 2:
                    wait("oev", u.group - 1)
                if u.kind in ("moba", "fox", "sb"):
                    rows = slice(u.half, u.half + HD)
                else:
                    rows = slice(0, P)
                dst = ps[rows, BO + u.group % 2, u.qt * P:(u.qt + 1) * P]
                for b in range(u.qt + 1):
                    if u.kind == "dsa":
                        vv = ckv_t[:, b, :]
                    elif u.kind == "diff":
                        vv = v2[:, b, 512 + u.h * P:512 + (u.h + 1) * P]
                    else:
                        vv = V[u.t][:, b, u.h * HD:(u.h + 1) * HD]
                    m = pe.matmul(dst, vv, PT[u.t][:, u.n % 2, b * P:(b + 1) * P],
                                  start=b == 0, stop=b == u.qt)
                m.then_inc(sem["pv"], 1)

            def forget_rows(h):
                wait("fg_dve", 4)
                if h:
                    wait("nc_ev", h)
                pe.matmul(ps[:, BX, :], sel8[:, h * P:(h + 1) * P], fg[:, 2, :], start=True,
                          stop=True).then_inc(sem["nc_mm"], 1)

            def absorb(h):
                if h:
                    wait("qa_ev", h)
                f = slice(HD * (h % 2), HD * (h % 2) + HD)
                pe.matmul(ps[:, BX, :], wuk[f, h // 2, :], qk3[f, 4 + h // 2, :], start=True,
                          stop=True).then_inc(sem["qa_mm"], 1)

            def attend(run):
                n, ahead = len(run), AHEAD[run[0].kind]
                kind = run[0].kind
                ends = {i: u for i, u in enumerate(run) if u.last}
                for i in range(-ahead, n + 4):
                    a = i + ahead
                    if a < n:
                        if run[a].qt == 0 and kind == "fox":
                            forget_rows(run[a].h)
                        if run[a].qt == 0 and kind == "dsa":
                            if run[a].h == 0:
                                absorb(0)
                            if run[a].h + 1 < HEADS and run[a].h == 0:
                                absorb(1)
                        if run[a].qt == 2 and kind == "dsa" and 1 <= run[a].h < HEADS - 1:
                            absorb(run[a].h + 1)
                        scores(run[a])
                    if 0 <= i < n:
                        turn(run[i])
                    if 1 <= i <= n:
                        values(run[i - 1])
                    if i - 3 in ends:
                        u = ends[i - 3]
                        if kind == "diff":
                            wait("df_sq", u.h + 1)
                            pe.matmul(ps[:, BX, :], ones, tmp[:, 0, :], start=True,
                                      stop=True).then_inc(sem["df_sum"], 1)
                        if kind == "dsa":
                            wait("ol_ev", u.h + 1)
                            rows = slice(u.half, u.half + HD)
                            pe.matmul(ps[rows, BO + u.group % 2, :], wuv[:, u.h * HD:(u.h + 1) * HD],
                                      olat[:, u.h % 2, :], start=True, stop=True).then_inc(sem["uv_mm"], 1)

            pe.wait_ge(sem["consts"], 64)
            pe.wait_ge(sem["bias_in"], 32)
            pe.matmul(ps[0:HEADS, 6, :], bb[:, :], oh[:, 0:512], start=True, stop=True)
            pe.matmul(ps[0:HEADS, 7, 0:P], bb[:, :], oh[:, 512:640], start=True,
                      stop=True).then_inc(sem["brow_mm"], 1)
            for c in range(DC):
                norm_sum(0, c)
            for j in range(10):
                project("in1", j, in_fill("norm0") if j == 0 else None, tokens=j >= 8)
            wait("qkv", 6)
            pe.wait_ge(sem["bias_out"], 16 * HEADS)
            attend(runs_of(1)[0])
            for stage in range(2):
                for c in range(4):
                    if stage == 0:
                        wait("taps", 4 * TAPS)
                        pe.matmul(ps[:, BX, :], ones, cacc[:, c, :], start=c == 0,
                                  stop=c == 3).then_inc(sem["ln_sum"], 1)
                    else:
                        wait("ln_dve", 4)
                        wait("ln_act", c + 1)
                        pe.matmul(ps[:, BX, :], ones, tmp[:, c, :], start=c == 0,
                                  stop=c == 3).then_inc(sem["ln_sum"], 1)
            out_proj("out1", "att1", 1)
            ffn_up("up1", "norm1")
            ffn_down("down1", 0, 2)

            for c in range(DC):
                norm_sum(3, c)
            wait("lam_dve", 1)
            pe.matmul(ps[:, 6, 0:2], sq_f[0:HD, 0, :], small[0:HD, 0:2], start=True,
                      stop=True).then_inc(sem["lam_mm"], 1)
            project("in2", 0, in_fill("norm3"), halves=(0,))
            for j in range(1, 6):
                project("in2", j)
            wait("fg_dve", 4)
            for t in range(QT):
                m = pe.transpose(ps[:, 7, t * 8:t * 8 + 8], fg[:, 1, t * P:(t + 1) * P],
                                 sq_f[0:HEADS, 1, 0:HEADS])
            m.then_inc(sem["cq_mm"], 1)
            for j in range(6, 10):
                project("in2", j, tokens=j >= 9)
                for r in (2 * (j - 6), 2 * (j - 6) + 1):
                    wait("qkv", QKV["in2"] + j)
                    rotate(2, r, 8 + r)
            for j in range(10, 13):
                project("in2", j, tokens=True)
            wait("qkv", QKV["in2"] + 13)
            wait("rope", 8)
            wait("cq_ev", 1)
            pe.wait_ge(sem["sel_in"], 16)
            for run in runs_of(2):
                attend(run)
            out_proj("out2", "att2", 4)
            ffn_up("up2", "norm4")
            ffn_down("down2", 1, 5)

            def latent():
                wait("kv_sq", 1)
                pe.matmul(ps[:, 6, :], ones, tmp[:, 2, :], start=True, stop=True).then_inc(sem["kv_sum"], 1)

            def index_logits():
                for b in range(1, QT):
                    for h in range(IDXH):
                        g = (b - 1) * IDXH + h
                        if g >= 2:
                            wait("lg_relu", g - 1)
                        f = slice(HD * (h % 2), HD * (h % 2) + HD)
                        pe.matmul(ps[:, 6 + g % 2, 0:P * (b + 1)], qk3[f, 2 + h // 2, b * P:(b + 1) * P],
                                  qk3[f, 1, 0:P * (b + 1)], start=True, stop=True).then_inc(sem["lg_mm"], 1)

            project("in3", 0, in_fill("norm5"))
            project("in3", 1)
            wait("qkv", QKV["in3"] + 1)
            for t in range(QT):
                m = pe.transpose(ps[:, 7, t * P:(t + 1) * P], qk3[:, 0, t * P:(t + 1) * P], ident)
            m.then_inc(sem["iw_tr"], 1)
            rotate(3, 8, 0)
            rotate(3, 9, 1)
            project("in3", 2, halves=(0,))
            wait("qkv", QKV["in3"] + 2)
            rotate(3, 10, 2)
            rotate(3, 11, 3)
            project("in3", 3)
            latent()
            wait("rope", 12)
            wait("kv_root", 1)
            wait("iw_ev", 1)
            index_logits()
            project("in3", 4)
            wait("qkv", QKV["in3"] + 4)
            rotate(3, 12, 4)
            rotate(3, 13, 5)
            wait("kv_dve", 2)
            wait("lg_relu", 12)
            for t in range(QT):
                m = pe.transpose(ps[:, 6, t * P:(t + 1) * P], ckv[:, t * P:(t + 1) * P], ident)
            m.then_inc(sem["kv_tr"], 1)
            project("in3", 5)
            wait("qkv", QKV["in3"] + 5)
            rotate(3, 14, 6)
            rotate(3, 15, 7)
            for j in range(6, 11):
                project("in3", j, tokens=j >= 9)
            wait("qkv", QKV["in3"] + 11)
            wait("rope", 16)
            wait("kv_ev", 1)
            attend(runs_of(3)[0])
            wait("selm", 4)
            pe.wait_ge(sem["l3_in"], 32)
            attend(runs_of(3)[1])
            out_proj("out3", "att3", 6)
            ffn_up("up3", "norm6")
            ffn_down("down3", 2, 7)

        @block.scalar
        def _(act):
            A = nc.scalar

            def wait(name, value):
                act.wait_ge(sem[name], value)

            def split(n):
                if n >= NSLAB:
                    return
                act.wait_ge(landed[n % 2], 16 * (n // 2 + 1))
                if n >= 2:
                    wait("slab", n - 1)
                A.copy(w_hi[:, n % 2, :], raw[:, n % 2, :]).then_inc(sem["whi"], 1)

            def squares_of(k, c):
                if k == 0:
                    act.wait_ge(sem["x_in"], 16 * DC)
                else:
                    wait("x", ready_x(k, c))
                if c >= 2:
                    wait("sums", DC * k + c - 1)
                A.activation(tmp[:, c % 2, :], xT[:, c, :], ACT.Square).then_inc(sem["sq"], 1)

            def root(k):
                wait("sums", DC * (k + 1))
                A.activation(tmp[:, 4, :], ps[:, BT, :], ACT.Sqrt, bias=col("eps"), scale=1.0 / D
                             ).then_inc(sem["root"], 1)

            def parts(name, a):
                for c in range(DC):
                    wait("u", DC * a + c + 1)
                    A.copy(a_hi[:, c, :], tmp[:, 2 + c % 2, :]).then_inc(sem["ahi"], 1)

            def out_phase(name, k):
                per = 3 if name.startswith("down") else 1
                for p in range(4):
                    for t in range(per):
                        if t == per - 1:
                            squares_of(k, 2 * p)
                            squares_of(k, 2 * p + 1)
                        split(BASE[name] + per * p + t + 2)

            def ffn_first():
                with act.Fori(0, FC // 2) as i:
                    for j in range(2):
                        n, o = BASE["up1"] + j, PAIR["up1"] + j
                        act.wait_ge(sem["slab"], i * 2 + (n + 1))
                        act.wait_ge(sem["wlo"], i * 2 + (n + 2))
                        A.activation(tmp[:, 2, :], ps[:, 2 * (o % 2), :], ACT.Silu).then_inc(sem["silu"], 1)
                        act.wait_ge(landed[n % 2], i * 16 + 16 * ((n + 2) // 2 + 1))
                        A.copy(w_hi[:, n % 2, :], raw[:, n % 2, :]).then_inc(sem["whi"], 1)
                        act.wait_ge(sem["h"], i * 2 + (j + 1))
                        A.copy(h_hi[:, i * 2 + j, :], tmp[:, 3 + j, :]).then_inc(sem["hhi"], 1)

            def ffn_conv(name, f):
                cols = COL["ffn2" if f == 1 else "ffn3"]
                with act.Fori(0, FC // 2) as i:
                    for j in range(2):
                        n, o = BASE[name] + j, PAIR[name] + j
                        act.wait_ge(sem["slab"], i * 2 + (n + 1))
                        act.wait_ge(sem["h"], i * 2 + (FC * f + j))
                        for g in range(2):
                            w = vec[:, bass.ds(i * 16 + (cols + 8 * j + 4 * g + 2), 1)]
                            b = vec[:, bass.ds(i * 16 + (cols + 8 * j + 4 * g + 3), 1)]
                            A.activation(tmp[:, g, :], ps[:, 2 * (o % 2) + g, :], ACT.Identity,
                                         bias=b, scale=w).then_inc(sem["lin"], 1)
                        act.wait_ge(landed[n % 2], i * 16 + 16 * ((n + 2) // 2 + 1))
                        A.copy(w_hi[:, n % 2, :], raw[:, n % 2, :]).then_inc(sem["whi"], 1)
                        act.wait_ge(sem["fconv"], i * 2 + (FC * (f - 1) + j + 1))
                        A.activation(tmp[:, 2, :], tmp[:, 0, :], ACT.Silu).then_inc(sem["silu"], 1)
                        act.wait_ge(sem["h"], i * 2 + (FC * f + j + 1))
                        A.copy(h_hi[:, i * 2 + j, :], tmp[:, 3, :]).then_inc(sem["hhi"], 1)

            def exps(u):
                for st in u.sets:
                    if u.kind == "sb":
                        wait("sc", st + 1)
                        z = ps[:, st % 3, 0:u.w]
                        t = SBI[u.t][:, st % 3, 0:u.w]
                        k = 3 * (u.sb - 1)
                        if st >= 3:
                            wait("ex", st - 2)
                            if u.sb >= 4:
                                wait("sb_dve", 3 * (u.sb - 3))
                        A.activation(t, z, ACT.Abs).then_inc(sem["sb_act"], 1)
                        wait("sb_act", k + 1)
                        A.activation(t, t, ACT.Exp, scale=-1.0).then_inc(sem["sb_act"], 1)
                        wait("sb_act", k + 2)
                        A.activation(t, t, ACT.Ln, bias=col("one")).then_inc(sem["sb_act"], 1)
                        continue
                    n_mx = u.mx - len(u.sets) + (st - u.sets[0]) + 1
                    wait("mx", n_mx)
                    if u.n >= 4:
                        wait("tr", u.n - 3 if len(u.sets) == 1 else u.n - 1)
                    src = SBI[u.t][:, st % 3, 0:u.w] if u.kind in ("moba", "fox") else ps[:, st % 3, 0:u.w]
                    A.activation(E[u.t][:, st % 4, 0:u.w], src, ACT.Exp, bias=stat[:, st % 4, 0:1],
                                 accum_out=stat[:, st % 4, 1:2]).then_inc(sem["ex"], 1)

            def sb_exp(u):
                st = u.sets[0]
                wait("sb_dve", 3 * u.sb)
                t = E[u.t][:, st % 4, 0:u.w]
                A.activation(t, t, ACT.Exp).then_inc(sem["ex"], 1)

            def move(u):
                wait("tr", u.n + 1)
                if u.n >= 2:
                    wait("pv", u.n - 1)
                A.copy(PT[u.t][:, u.n % 2, 0:u.w], ps[:, BT + u.n % 2, 0:u.w]).then_inc(sem["pt"], 1)

            def out_chunk(u):
                if u.kind == "diff":
                    return 4 + u.h, slice(0, P)
                if u.kind == "dsa":
                    return u.h // 2, slice(u.half, u.half + HD)
                return (4 if u.kind == "sb" else 0) + u.h // 2, slice(0, P)

            def attend(run):
                n, ahead = len(run), AHEAD[run[0].kind]
                kind = run[0].kind
                ends = {i: u for i, u in enumerate(run) if u.last}
                for i in range(-ahead, n + 5):
                    a = i + ahead
                    if a < n:
                        h = run[a].h
                        if run[a].qt == 0 and kind == "fox":
                            wait("nc_mm", h + 1)
                            if h >= 2:
                                wait("bs", run[a].bs - 1 - 4)
                            A.copy(ncb[:, h % 2, :], ps[:, BX, :]).then_inc(sem["nc_ev"], 1)
                        if kind == "dsa":
                            todo = []
                            if run[a].qt == 0 and h == 0:
                                todo = [0, 1]
                            if run[a].qt == 2 and 1 <= h < HEADS - 1:
                                todo = [h + 1]
                            for hh in todo:
                                wait("qa_mm", hh + 1)
                                if hh >= 2:
                                    wait("sc", run[4 * (hh - 1) - 1].sets[0] + 1)
                                A.copy(qabs[:, hh % 2, :], ps[:, BX, :]).then_inc(sem["qa_ev"], 1)
                        exps(run[a])
                    if kind == "sb" and 0 <= a - 1 < n:
                        sb_exp(run[a - 1])
                    if 0 <= i < n:
                        move(run[i])
                    if kind in ("moba", "fox", "sb") and i - 2 in ends:
                        u = ends[i - 2]
                        wait("pv", u.n + 1)
                        A.copy(a_hi[:, out_chunk(u)[0], :], ps[:, BO + u.group % 2, :]).then_inc(sem["ahi"], 1)
                    if kind == "diff":
                        if i - 2 in ends:
                            u = ends[i - 2]
                            wait("pv", u.n + 1)
                            if u.h:
                                wait("df_sum", u.h)
                            A.activation(tmp[:, 0, :], ps[:, BO + u.group % 2, :], ACT.Square
                                         ).then_inc(sem["df_sq"], 1)
                        if i - 4 in ends:
                            u = ends[i - 4]
                            wait("df_sum", u.h + 1)
                            if u.h:
                                wait("df_rec", u.h)
                            A.activation(tmp[:, 1, :], ps[:, BX, :], ACT.Sqrt, bias=col("eps"),
                                         scale=1.0 / P).then_inc(sem["df_root"], 1)
                            wait("oev", u.group + 1)
                            A.copy(a_hi[:, out_chunk(u)[0], :], tmp[:, 3, :]).then_inc(sem["ahi"], 1)
                    if kind == "dsa":
                        if i - 2 in ends:
                            u = ends[i - 2]
                            wait("pv", u.n + 1)
                            if u.h >= 2:
                                wait("uv_mm", u.h - 1)
                            A.copy(olat[:, u.h % 2, :], ps[:, BO + u.group % 2, :]).then_inc(sem["ol_ev"], 1)
                        if i - 4 in ends:
                            u = ends[i - 4]
                            chunk, rows = out_chunk(u)
                            wait("uv_mm", u.h + 1)
                            A.copy(a_hi[rows, chunk, :], ps[rows, BO + u.group % 2, :]).then_inc(sem["ahi"], 1)

            for c in range(DC):
                squares_of(0, c)
            act.wait_ge(sem["consts"], 64)
            wait("rope_dve", 1)
            root(0)
            split(0)
            parts("norm0", 0)
            split(1)
            wait("rope_dve", 7)
            A.activation(sinT[:, :], cosT[:, :], ACT.Sin).then_inc(sem["rope_act"], 1)
            A.activation(tmp[:, 1, :], cosT[:, :], ACT.Abs).then_inc(sem["rope_act"], 1)
            wait("rope_act", 2)
            A.activation(cosT[:, :], tmp[:, 1, :], ACT.Sin, bias=col("half_pi"), scale=-1.0
                         ).then_inc(sem["rope_act"], 1)

            for j in range(10):
                n, o = BASE["in1"] + j, PAIR["in1"] + j
                if j < 4:
                    wait("slab", n + 1)
                    if j == 0:
                        wait("rope_act", 3)
                    else:
                        wait("glu", j)
                    A.activation(tmp[:, 0, :], ps[:, 2 * (o % 2) + 1, :], ACT.Sigmoid).then_inc(sem["glu_g"], 1)
                split(n + 2)
            attend(runs_of(1)[0])
            for c in range(4):
                wait("ln_dve", c + 1)
                A.activation(tmp[:, c, :], cacc[:, c, :], ACT.Square).then_inc(sem["ln_act"], 1)
            wait("ln_sum", 8)
            A.activation(tmp[:, 4, :], ps[:, BX, :], ACT.Sqrt, bias=col("ln_eps"), scale=1.0 / 512
                         ).then_inc(sem["ln_act"], 1)
            for c in range(4):
                wait("ln_dve", 6 + c)
                A.activation(tmp[:, c, :], cacc[:, c, :], ACT.Silu, bias=col("ln_b", c),
                             scale=col("ln_g", c)).then_inc(sem["ln_act"], 1)
                wait("ln_act", 6 + c)
                A.copy(a_hi[:, 4 + c, :], tmp[:, c, :]).then_inc(sem["ahi"], 1)
            out_phase("out1", 1)
            root(1)
            parts("norm1", 1)
            ffn_first()
            out_phase("down1", 2)
            root(2)

            for c in range(DC):
                squares_of(3, c)
            root(3)
            parts("norm3", 2)
            wait("lam_mm", 1)
            A.activation(small[:, 2:4], ps[:, 6, 0:2], ACT.Exp).then_inc(sem["lam_act"], 1)
            for j in range(13):
                split(BASE["in2"] + j + 2)
                if j == 0:
                    wait("fg_dve", 1)
                    A.activation(fg[:, 1, :], fg[:, 0, :], ACT.Abs).then_inc(sem["fg_act"], 1)
                    wait("fg_act", 1)
                    A.activation(fg[:, 1, :], fg[:, 1, :], ACT.Exp, scale=-1.0).then_inc(sem["fg_act"], 1)
                    wait("fg_act", 2)
                    A.activation(fg[:, 1, :], fg[:, 1, :], ACT.Ln, bias=vec[0:HEADS, COL["one"]:COL["one"] + 1]
                                 ).then_inc(sem["fg_act"], 1)
            for run in runs_of(2):
                attend(run)
            out_phase("out2", 4)
            root(4)
            parts("norm4", 3)
            ffn_conv("up2", 1)
            out_phase("down2", 5)
            root(5)
            parts("norm5", 4)

            for j in range(11):
                split(BASE["in3"] + j + 2)
                if j == 2:
                    wait("qkv", QKV["in3"] + 3)
                    A.activation(tmp[:, 2, :], ckv[:, :], ACT.Square).then_inc(sem["kv_sq"], 1)
                if j == 3:
                    wait("kv_sum", 1)
                    A.activation(tmp[:, 4, :], ps[:, 6, :], ACT.Sqrt, bias=col("eps"), scale=1.0 / RANK
                                 ).then_inc(sem["kv_root"], 1)
                    for g in range(12):
                        b = 1 + g // IDXH
                        wait("lg_mm", g + 1)
                        if g >= 2:
                            wait("score", 3 + g - 1)
                        A.activation(tmp[:, g % 2, 0:P * (b + 1)], ps[:, 6 + g % 2, 0:P * (b + 1)], ACT.Relu
                                     ).then_inc(sem["lg_relu"], 1)
                if j == 4:
                    wait("kv_tr", 1)
                    A.copy(ckv_t[:, :, :], ps[:, 6, :].rearrange("p (t r) -> p t r", t=QT)).then_inc(sem["kv_ev"], 1)
            for run in runs_of(3):
                attend(run)
            out_phase("out3", 6)
            root(6)
            parts("norm6", 5)
            ffn_conv("up3", 2)
            out_phase("down3", 7)
            root(7)

        @block.vector
        def _(dve):
            Vv = nc.vector

            def wait(name, value):
                dve.wait_ge(sem[name], value)

            def split(n):
                if n >= NSLAB:
                    return
                wait("whi", n + 1)
                Vv.tensor_tensor(w_lo[:, n % 2, :], raw[:, n % 2, :], w_hi[:, n % 2, :].bitcast(F32),
                                 ALU.subtract).then_inc(sem["wlo"], 1)

            def reciprocal_root(k):
                wait("root", k + 1)
                Vv.reciprocal(tmp[:, 5, :], tmp[:, 4, :]).then_inc(sem["rstd"], 1)
                wait("rstd", k + 1)

            def low(c, src, n):
                wait("ahi", n)
                Vv.tensor_tensor(a_lo[:, c, :], src, a_hi[:, c, :].bitcast(F32), ALU.subtract
                                 ).then_inc(sem["alo"], 1)

            def normed(k, name, a):
                reciprocal_root(k)
                for c in range(DC + 1):
                    if c < DC:
                        if c >= 2:
                            wait("alo", LOWS[name] + c - 1)
                        Vv.scalar_tensor_tensor(out=tmp[:, 2 + c % 2, :], in0=xT[:, c, :],
                                                scalar=col("gain", DC * k + c), in1=tmp[:, 5, :],
                                                op0=ALU.mult, op1=ALU.mult).then_inc(sem["u"], 1)
                    if c:
                        low(c - 1, tmp[:, 2 + (c - 1) % 2, :], FILL[name] + c)

            def normed_residual(k):
                reciprocal_root(k)
                for c in range(DC):
                    Vv.scalar_tensor_tensor(out=xT[:, c, :], in0=xT[:, c, :],
                                            scalar=col("gain", DC * k + c), in1=tmp[:, 5, :],
                                            op0=ALU.mult, op1=ALU.mult).then_inc(sem["x"], 1)

            def out_phase(name):
                per = 3 if name.startswith("down") else 1
                for p in range(4):
                    for t in range(per):
                        n = BASE[name] + per * p + t
                        if t == per - 1:
                            wait("slab", n + 1)
                            bank = 2 * ((PAIR[name] + p) % 2)
                            for half in range(2):
                                c = 2 * p + half
                                Vv.tensor_tensor(xT[:, c, :], xT[:, c, :], ps[:, bank + half, :], ALU.add
                                                 ).then_inc(sem["x"], 1)
                        split(n + 2)

            def ffn_first():
                with dve.Fori(0, FC // 2) as i:
                    for j in range(2):
                        n, o = BASE["up1"] + j, PAIR["up1"] + j
                        dve.wait_ge(sem["silu"], i * 2 + (j + 1))
                        Vv.tensor_tensor(tmp[:, 3 + j, :], tmp[:, 2, :], ps[:, 2 * (o % 2) + 1, :], ALU.mult
                                         ).then_inc(sem["h"], 1)
                        dve.wait_ge(sem["whi"], i * 2 + (n + 3))
                        Vv.tensor_tensor(w_lo[:, n % 2, :], raw[:, n % 2, :], w_hi[:, n % 2, :].bitcast(F32),
                                         ALU.subtract).then_inc(sem["wlo"], 1)
                        dve.wait_ge(sem["hhi"], i * 2 + (j + 1))
                        Vv.tensor_tensor(h_lo[:, i * 2 + j, :], tmp[:, 3 + j, :],
                                         h_hi[:, i * 2 + j, :].bitcast(F32), ALU.subtract
                                         ).then_inc(sem["hlo"], 1)

            def ffn_conv(name, f):
                cols = COL["ffn2" if f == 1 else "ffn3"]
                with dve.Fori(0, FC // 2) as i:
                    for j in range(2):
                        n, o = BASE[name] + j, PAIR[name] + j
                        for tap in (1, 0):
                            for g in range(2):
                                if tap == 1:
                                    dve.wait_ge(sem["lin"], i * 4 + (2 * (FC * (f - 1) + j) + g + 1))
                                else:
                                    dve.wait_ge(sem["fstep"], i * 4 + (2 * (FC * (f - 1) + j) + g + 1))
                                w = vec[:, bass.ds(i * 16 + (cols + 8 * j + 4 * g + tap), 1)]
                                lag = 2 - tap
                                step = Vv.scalar_tensor_tensor(
                                    out=tmp[:, g, lag:S], in0=ps[:, 2 * (o % 2) + g, 0:S - lag], scalar=w,
                                    in1=tmp[:, g, lag:S], op0=ALU.mult, op1=ALU.add)
                                if tap == 1:
                                    step.then_inc(sem["fstep"], 1)
                        step.then_inc(sem["fconv"], 1)
                        dve.wait_ge(sem["whi"], i * 2 + (n + 3))
                        Vv.tensor_tensor(w_lo[:, n % 2, :], raw[:, n % 2, :], w_hi[:, n % 2, :].bitcast(F32),
                                         ALU.subtract).then_inc(sem["wlo"], 1)
                        dve.wait_ge(sem["silu"], i * 2 + (FC * f + j + 1))
                        Vv.tensor_tensor(tmp[:, 3, :], tmp[:, 2, :], tmp[:, 1, :], ALU.mult).then_inc(sem["h"], 1)
                        dve.wait_ge(sem["hhi"], i * 2 + (FC * f + j + 1))
                        Vv.tensor_tensor(h_lo[:, i * 2 + j, :], tmp[:, 3, :],
                                         h_hi[:, i * 2 + j, :].bitcast(F32), ALU.subtract
                                         ).then_inc(sem["hlo"], 1)

            done_taps = [0]

            def taps(count):
                for _ in range(count):
                    k = done_taps[0]
                    if k == 4 * TAPS:
                        return
                    j, c = k // 4, k % 4
                    src = cu[:, c, j:j + S]
                    if j == 0:
                        wait("glu", c + 1)
                        Vv.tensor_scalar(cacc[:, c, :], src, col("conv_w", c * TAPS), col("conv_b", c),
                                         ALU.mult, ALU.add).then_inc(sem["taps"], 1)
                    else:
                        wait("taps", k - 3)
                        Vv.scalar_tensor_tensor(out=cacc[:, c, :], in0=src, scalar=col("conv_w", c * TAPS + j),
                                                in1=cacc[:, c, :], op0=ALU.mult, op1=ALU.add
                                                ).then_inc(sem["taps"], 1)
                    done_taps[0] += 1

            def move_features(name, j, dst, scale, halves=2):
                n, o = BASE[name] + j, PAIR[name] + j
                wait("slab", n + 1)
                bank = 2 * (o % 2)
                Vv.tensor_scalar(dst, ps[:, bank:bank + halves, :], scale, None, ALU.mult
                                 ).then_inc(sem["qkv"], 1)

            def move_tokens(name, j, v, c0):
                n, o = BASE[name] + j, PAIR[name] + j
                wait("slab", n + 1)
                bank = 2 * (o % 2)
                Vv.tensor_copy(v[:, :, c0:c0 + 256], ps[:, bank:bank + 2, :].rearrange(
                    "p b (t c) -> p (b t) c", c=256)).then_inc(sem["qkv"], 1)

            def rope(t, r, chunk):
                x = QK[t][:, chunk, :]
                sc = SBI[t][:, r % 2, :]
                wait("rot", r + 1)
                Vv.tensor_tensor(sc, ps[:, BT + r % 2, :], sinT[:, :], ALU.mult).then_inc(sem["rope_t"], 1)
                Vv.tensor_tensor(x, x, cosT[:, :], ALU.mult).then_inc(sem["rope_c"], 1)
                wait("rope_t", r + 1)
                wait("rope_c", r + 1)
                Vv.tensor_tensor(x, x, sc, ALU.add).then_inc(sem["rope"], 1)

            def biased(u):
                st = u.sets[0]
                dst = SBI[u.t][:, st % 3, 0:u.w]
                src = ps[:, st % 3, 0:u.w]
                wait("sc", st + 1)
                if u.kind == "moba":
                    Vv.scalar_tensor_tensor(out=dst, in0=src, scalar=SCALE,
                                            in1=bias_t[:, u.h, S - P - P * u.qt:S], op0=ALU.mult,
                                            op1=ALU.add).then_inc(sem["bs"], 1)
                else:
                    wait("nc_ev", u.h + 1)
                    Vv.scalar_tensor_tensor(out=dst, in0=ncb[:, u.h % 2, 0:u.w],
                                            scalar=cq_t[:, u.qt, u.h:u.h + 1], in1=src, op0=ALU.add,
                                            op1=ALU.add).then_inc(sem["bs"], 1)

            def maxima(u):
                for j, st in enumerate(u.sets):
                    if u.kind in ("moba", "fox"):
                        biased(u)
                        wait("bs", u.bs)
                        src = SBI[u.t][:, st % 3, 0:u.w]
                    else:
                        wait("sc", st + 1)
                        src = ps[:, st % 3, 0:u.w]
                    Vv.tensor_reduce(stat[:, st % 4, 0:1], src, AX.X, ALU.max, negate=True
                                     ).then_inc(sem["mx"], 1)

            def sb_sums(u):
                st = u.sets[0]
                z = ps[:, st % 3, 0:u.w]
                t = SBI[u.t][:, st % 3, 0:u.w]
                e = E[u.t][:, st % 4, 0:u.w]
                k = 3 * (u.sb - 1)
                wait("sb_act", k + 3)
                Vv.scalar_tensor_tensor(out=t, in0=z, scalar=0.0, in1=t, op0=ALU.max, op1=ALU.add
                                        ).then_inc(sem["sb_dve"], 1)
                wait("sb_dve", k + 1)
                if u.n >= 4:
                    wait("tr", u.n - 3)
                Vv.tensor_tensor_scan(e[:, ::-1], t[:, ::-1], t[:, ::-1], 0.0, ALU.add, ALU.bypass
                                      ).then_inc(sem["sb_dve"], 1)
                wait("sb_dve", k + 2)
                Vv.tensor_tensor(e, z, e, ALU.subtract).then_inc(sem["sb_dve"], 1)

            def factors(u):
                a = u.sets[0]
                e = E[u.t][:, a % 4, 0:u.w]
                k = 2 * (u.pr - 1)
                wait("ex", u.sets[-1] + 1)
                if u.kind != "diff":
                    Vv.reciprocal(stat[:, a % 4, 2:3], stat[:, a % 4, 1:2]).then_inc(sem["fac"], 2)
                    wait("fac", k + 2)
                    Vv.tensor_scalar(e, e, stat[:, a % 4, 2:3], None, ALU.mult).then_inc(sem["pr"], 1)
                    return
                b = u.sets[1]
                e2 = E[u.t][:, b % 4, 0:u.w]
                Vv.reciprocal(stat[:, a % 4, 2:3], stat[:, a % 4, 1:2])
                Vv.reciprocal(stat[:, b % 4, 2:3], stat[:, b % 4, 1:2]).then_inc(sem["fac"], 1)
                wait("fac", k + 1)
                Vv.tensor_scalar(e2, e2, stat[:, b % 4, 2:3], small[:, 5:6], ALU.mult, ALU.mult
                                 ).then_inc(sem["fac"], 1)
                wait("fac", k + 2)
                Vv.scalar_tensor_tensor(out=e, in0=e, scalar=stat[:, a % 4, 2:3], in1=e2, op0=ALU.mult,
                                        op1=ALU.add).then_inc(sem["pr"], 1)

            fills = {"att1": 0, "att2": 0, "att3": 0}

            def attend(run, spare=lambda: None):
                n, ahead = len(run), AHEAD[run[0].kind]
                kind, t = run[0].kind, run[0].t
                ends = {i: u for i, u in enumerate(run) if u.last}
                name = f"att{t}"
                for i in range(-ahead, n + 5):
                    a = i + ahead
                    if a < n:
                        if kind == "sb":
                            sb_sums(run[a])
                        else:
                            maxima(run[a])
                    if kind != "sb" and 0 <= a - 1 < n:
                        factors(run[a - 1])
                    if 0 <= i < n:
                        spare()
                    if kind in ("moba", "fox", "sb") and i - 2 in ends:
                        u = ends[i - 2]
                        fills[name] += 1
                        c = (4 if kind == "sb" else 0) + u.h // 2
                        wait("ahi", FILL[name] + fills[name])
                        Vv.tensor_tensor(a_lo[:, c, :], ps[:, BO + u.group % 2, :],
                                         a_hi[:, c, :].bitcast(F32), ALU.subtract).then_inc(sem["oev"], 1)
                        wait("oev", u.group + 1)
                    if kind == "diff" and i - 4 in ends:
                        u = ends[i - 4]
                        fills[name] += 1
                        wait("df_root", u.h + 1)
                        Vv.reciprocal(tmp[:, 2, :], tmp[:, 1, :]).then_inc(sem["df_rec"], 1)
                        wait("df_rec", u.h + 1)
                        Vv.scalar_tensor_tensor(out=tmp[:, 3, :], in0=ps[:, BO + u.group % 2, :],
                                                scalar=small[:, 6:7], in1=tmp[:, 2, :], op0=ALU.mult,
                                                op1=ALU.mult).then_inc(sem["oev"], 1)
                        low(4 + u.h, tmp[:, 3, :], FILL[name] + fills[name])
                    if kind == "dsa" and i - 4 in ends:
                        u = ends[i - 4]
                        fills[name] += 1
                        rows, c = slice(u.half, u.half + HD), u.h // 2
                        wait("ahi", FILL[name] + fills[name])
                        Vv.tensor_tensor(a_lo[rows, c, :], ps[rows, BO + u.group % 2, :],
                                         a_hi[rows, c, :].bitcast(F32), ALU.subtract).then_inc(sem["oev"], 1)
                        wait("oev", u.group + 1)
                E_ = None

            dve.wait_ge(sem["consts"], 64)
            Vv.tensor_copy(sq_b[:, 0, :], ident)
            Vv.tensor_copy(sq_b[:, 1:3, :], tmp[:, 5, 0:2 * P].rearrange("p (a b) -> p a b", a=2)
                           ).then_inc(sem["masks"], 1)
            wait("masks", 1)
            Vv.memset(cu[:, :, 0:PADL], 0.0).then_inc(sem["pad"], 1)
            n_rope = 0
            pos, ang = sinT[:, :], cosT[:, :]

            def rope_step(ins):
                ins.then_inc(sem["rope_dve"], 1)

            rope_step(Vv.tensor_copy(pos, tmp[:, 4, :].bitcast(I32)))
            wait("rope_dve", 1)
            rope_step(Vv.tensor_scalar(ang, pos, col("freq"), None, ALU.mult))
            wait("rope_dve", 2)
            wait("brow_mm", 1)
            Vv.tensor_copy(brow[:, 0:512], ps[0:HEADS, 6, :]).then_inc(sem["brow_ev"], 1)
            Vv.tensor_copy(brow[:, 512:640], ps[0:HEADS, 7, 0:P]).then_inc(sem["brow_ev"], 1)
            normed(0, "norm0", 0)
            split(0)
            split(1)
            turns = tmp[:, 0, :]
            rope_step(Vv.tensor_scalar(turns, ang, 1.0 / (2 * math.pi), MAGIC, ALU.mult, ALU.add))
            wait("rope_dve", 3)
            Vv.tensor_scalar(turns, turns, MAGIC, None, ALU.subtract).then_inc(sem["pad"], 1)
            wait("pad", 2)
            for part, value in enumerate(TWO_PI):
                rope_step(Vv.scalar_tensor_tensor(out=ang, in0=turns, scalar=-value, in1=ang,
                                                  op0=ALU.mult, op1=ALU.add))
                wait("rope_dve", 4 + part)
            rope_step(Vv.tensor_scalar(ang, ang, 3.1415925, -3.1415925, ALU.min, ALU.max))
            wait("rope_dve", 7)
            wait("rope_act", 3)

            for j in range(10):
                o = PAIR["in1"] + j
                if j < 4:
                    wait("glu_g", j + 1)
                    Vv.tensor_tensor(cu[:, j, PADL:PADL + S], ps[:, 2 * (o % 2), :], tmp[:, 0, :], ALU.mult
                                     ).then_inc(sem["glu"], 1)
                elif j < 8:
                    move_features("in1", j, qk1[:, 2 * (j - 4):2 * (j - 4) + 2, :], 1.0)
                else:
                    move_tokens("in1", j, v1, 256 * (j - 8))
                split(BASE["in1"] + j + 2)
                if j >= 4:
                    taps(12)
            attend(runs_of(1)[0], lambda: taps(2))
            wait("ln_sum", 4)
            for c in range(4):
                Vv.scalar_tensor_tensor(out=cacc[:, c, :], in0=ps[:, BX, :], scalar=-1.0 / 512,
                                        in1=cacc[:, c, :], op0=ALU.mult, op1=ALU.add).then_inc(sem["ln_dve"], 1)
            wait("ln_act", 5)
            Vv.reciprocal(tmp[:, 5, :], tmp[:, 4, :]).then_inc(sem["ln_dve"], 1)
            wait("ln_dve", 5)
            for c in range(4):
                Vv.tensor_tensor(cacc[:, c, :], cacc[:, c, :], tmp[:, 5, :], ALU.mult).then_inc(sem["ln_dve"], 1)
            for c in range(4):
                low(4 + c, tmp[:, c, :], FILL["att1"] + 5 + c)
            out_phase("out1")
            normed(1, "norm1", 1)
            ffn_first()
            out_phase("down1")
            normed_residual(2)

            normed(3, "norm3", 2)
            lam = vec[0:HD, COL["lam"]:COL["lam"] + 4]
            Vv.tensor_tensor(small[0:HD, 0:2], lam[:, 0:2], lam[:, 2:4], ALU.mult).then_inc(sem["lam_dve"], 1)
            wait("lam_act", 1)
            Vv.tensor_tensor(small[:, 4:5], small[:, 3:4], small[:, 2:3], ALU.subtract).then_inc(sem["lam_dve"], 1)
            wait("lam_dve", 2)
            Vv.tensor_scalar(small[:, 5:6], small[:, 4:5], -LAM_INIT, None, ALU.add)
            Vv.tensor_scalar(small[:, 6:7], col("subln"), 1.0 - LAM_INIT, None, ALU.mult).then_inc(sem["lam_dve"], 1)
            wait("lam_dve", 3)
            for j in range(13):
                n, o = BASE["in2"] + j, PAIR["in2"] + j
                if j == 0:
                    wait("slab", n + 1)
                    Vv.tensor_scalar(fg[:, 0, :], ps[0:HEADS, 2 * (o % 2), :],
                                     vec[0:HEADS, COL["fgate_b"]:COL["fgate_b"] + 1], None, ALU.add
                                     ).then_inc(sem["qkv"], 1)
                    wait("qkv", QKV["in2"] + 1)
                    Vv.tensor_scalar(fg[:, 2, :], fg[:, 0, :], 0.0, None, ALU.min).then_inc(sem["fg_dve"], 1)
                elif j < 9:
                    move_features("in2", j, qk2[:, 2 * (j - 1):2 * (j - 1) + 2, :],
                                  SCALE if j in (1, 2, 5, 6) else 1.0)
                else:
                    move_tokens("in2", j, v2, 256 * (j - 9))
                split(n + 2)
                if j == 1:
                    wait("fg_act", 3)
                    Vv.tensor_tensor(fg[:, 2, :], fg[:, 2, :], fg[:, 1, :], ALU.subtract).then_inc(sem["fg_dve"], 1)
                    wait("fg_dve", 2)
                    Vv.tensor_tensor_scan(fg[:, 1, :], fg[:, 2, :], fg[:, 2, :], 0.0, ALU.add, ALU.bypass
                                          ).then_inc(sem["fg_dve"], 1)
                    wait("fg_dve", 3)
                    Vv.tensor_scalar(fg[:, 2, :], fg[:, 1, :], -1.0, None, ALU.mult).then_inc(sem["fg_dve"], 1)
                if 6 <= j < 10:
                    for r in (2 * (j - 6), 2 * (j - 6) + 1):
                        rope(2, r, 8 + r)
                if j == 10:
                    wait("cq_mm", 1)
                    Vv.tensor_copy(cq_t[:, :, :], ps[:, 7, 0:QT * 8].rearrange("p (t h) -> p t h", h=HEADS)
                                   ).then_inc(sem["cq_ev"], 1)
                    wait("cq_ev", 1)
            for run in runs_of(2):
                attend(run)
            out_phase("out2")
            normed(4, "norm4", 3)
            ffn_conv("up2", 1)
            out_phase("down2")
            normed(5, "norm5", 4)

            done_top = [0]

            def top_rounds(count):
                for _ in range(count):
                    r = done_top[0]
                    if r == TOPK // 8:
                        return
                    for b in range(3):
                        if r:
                            wait("topr", 3 * (r - 1) + b + 1)
                        Vv.max(max8[:, b, :], score[:, b, 0:P * (b + 2)]).then_inc(sem["top8"], 1)
                    for b in range(3):
                        wait("top8", 3 * r + b + 1)
                        Vv.match_replace(score[:, b, 0:P * (b + 2)], max8[:, b, :], score[:, b, 0:P * (b + 2)],
                                         TAKEN).then_inc(sem["topr"], 1)
                    done_top[0] += 1

            def index_scores():
                wait("iw_tr", 1)
                Vv.tensor_scalar(iwq[:, :, :], ps[:, 7, :].rearrange("p (t f) -> p t f", f=P)[:, :, 32:36],
                                 IDXH ** -0.5, None, ALU.mult).then_inc(sem["iw_ev"], 1)
                for b in range(3):
                    Vv.memset(score[:, b, 0:P * (b + 1)], 0.0)
                    Vv.tensor_copy(score[:, b, P * (b + 1):P * (b + 2)], tri_b).then_inc(sem["score"], 1)

            def add_heads():
                wait("iw_ev", 1)
                for g in range(12):
                    b, h = g // IDXH, g % IDXH
                    wait("lg_relu", g + 1)
                    wait("score", 3 + g)
                    dst = score[:, b, 0:P * (b + 2)]
                    Vv.scalar_tensor_tensor(out=dst, in0=tmp[:, g % 2, 0:P * (b + 2)],
                                            scalar=iwq[:, b + 1, h:h + 1], in1=dst, op0=ALU.mult,
                                            op1=ALU.add).then_inc(sem["score"], 1)

            for j in range(11):
                if j == 0:
                    move_features("in3", 0, qk3[:, 0:2, :], 1.0)
                elif j == 1:
                    move_features("in3", 1, qk3[:, 2:4, :], 1.0)
                elif j == 2:
                    move_features("in3", 2, ckv[:, :].unsqueeze(1), 1.0, halves=1)
                elif j < 9:
                    move_features("in3", j, qk3[:, 2 * (j - 3) + 4:2 * (j - 3) + 6, :],
                                  1.0 if j >= 7 else SCALE)
                else:
                    move_tokens("in3", j, v3, 256 * (j - 9))
                split(BASE["in3"] + j + 2)
                if j == 1:
                    index_scores()
                    rope(3, 8, 0)
                    wait("rope", 9)
                    Vv.tensor_scalar(qk3[:, 0, :], qk3[:, 0, :], col("rope_rows"), None, ALU.mult
                                     ).then_inc(sem["kv_dve"], 1)
                    rope(3, 9, 1)
                if j == 2:
                    rope(3, 10, 2)
                    rope(3, 11, 3)
                if j == 3:
                    wait("kv_root", 1)
                    Vv.reciprocal(tmp[:, 5, :], tmp[:, 4, :]).then_inc(sem["pad"], 1)
                    wait("pad", 3)
                    Vv.scalar_tensor_tensor(out=ckv[:, :], in0=ckv[:, :], scalar=col("kv_norm"),
                                            in1=tmp[:, 5, :], op0=ALU.mult, op1=ALU.mult
                                            ).then_inc(sem["kv_dve"], 1)
                    add_heads()
                if j == 4:
                    rope(3, 12, 4)
                    rope(3, 13, 5)
                if j == 5:
                    rope(3, 14, 6)
                    rope(3, 15, 7)
                if j >= 4:
                    top_rounds(2)
            attend(runs_of(3)[0], lambda: top_rounds(1))
            top_rounds(TOPK // 8)
            wait("topr", 3 * TOPK // 8)
            Vv.tensor_copy(selm[:, 0, 0:P], tri_b).then_inc(sem["selm"], 1)
            for b in range(3):
                Vv.tensor_scalar(selm[:, b + 1, 0:P * (b + 2)], score[:, b, 0:P * (b + 2)], TAKEN / 2, NEG,
                                 ALU.is_gt, ALU.mult).then_inc(sem["selm"], 1)
            attend(runs_of(3)[1])
            out_phase("out3")
            normed(6, "norm6", 5)
            ffn_conv("up3", 2)
            out_phase("down3")
            normed_residual(7)


def bucket_rows():
    dist = 511 - np.arange(640)
    d = np.maximum(dist, 1).astype(np.float64)
    large = 16 + (np.log(d / 16) / math.log(8.0) * 16).astype(np.int64)
    bucket = np.where(dist < 16, dist, np.minimum(large, 31))
    bucket = np.where(dist < 0, 32, bucket)
    return (np.arange(33)[:, None] == bucket[None, :]).astype(np.float32)


def square_tables():
    i = np.arange(P)
    rot = np.zeros((P, P), np.float32)
    for base in (0, 64):
        for r in range(8):
            rot[base + 8 + r, base + r] = -1.0
            rot[base + r, base + 8 + r] = 1.0
    after = np.where(i[None, :] > i[:, None], np.float32(NEG), np.float32(0))
    own = np.where(i[None, :] >= i[:, None], np.float32(NEG), np.float32(0))
    return np.stack([np.ones((P, P)), np.eye(P), rot, after, own], axis=1).astype(np.float32)


def slabs(w, columns):
    K = w.shape[0]
    w = np.concatenate([w, np.zeros((K, 1), np.float32)], axis=1)
    out = []
    for cols in columns:
        cols = np.concatenate([cols, np.full(256 - len(cols), -1)]).astype(np.int64)
        out.append(w[:, cols].reshape(K // P, P, 256).transpose(1, 0, 2))
    return out


def pack_weights(w_in, w_out, w_gate, w_up, w_down, ev_in, ev_out, od_in, od_out, ffn_in, ffn_out):
    r = lambda a, n: np.arange(a, a + n)
    none = lambda n: np.full(n, -1)
    every = [r(256 * j, 256) for j in range(4)]
    res = []

    def down(w):
        for full in slabs(w, every):
            for k0 in (0, 8, 16):
                part = full[:, k0:k0 + 8]
                if part.shape[1] < 8:
                    part = np.concatenate([part, np.zeros((P, 8 - part.shape[1], 256), np.float32)], axis=1)
                res.append(part)

    res += slabs(w_in, [np.concatenate([r(1536 + P * j, P), r(2048 + P * j, P)]) for j in range(4)]
                 + [r(256 * j, 256) for j in range(6)])
    res += slabs(w_out, every)
    both = np.concatenate([w_gate, w_up], axis=1)
    halves = [np.concatenate([r(P * j, P), r(FF + P * j, P)]) for j in range(FC)]
    res += slabs(both, halves)
    down(w_down)
    c = 3 * 512 + 8
    res += slabs(ev_in, [r(1536, 8)] + [r(256 * j, 256) for j in range(4)]
                 + [r(c + 256 * j, 256) for j in range(4)]
                 + [r(1024, 256), r(1280, 256), r(c + 1024, 256), r(c + 1280, 256)])
    res += slabs(ev_out, every)
    res += slabs(ffn_in[0], halves)
    down(ffn_out[0])
    ckv, ckr, ciq, ciw, cik, sq = 512, 640, 656, 912, 916, 980
    res += slabs(od_in, [
        np.concatenate([r(ckr, 16), none(16), r(ciw, 4), none(28), r(ckr, 16), none(48), r(cik, 64), r(cik, 64)]),
        r(ciq, 256), r(ckv, 128), r(0, 256), r(256, 256)] + [r(sq + 256 * j, 256) for j in range(6)])
    res += slabs(od_out, every)
    res += slabs(ffn_in[1], halves)
    down(ffn_out[1])
    return np.stack(res).reshape(len(res), P, 2048)


def pack_vectors(gains, conv_w, conv_b, ln_g, ln_b, ffn_w, ffn_b, subln, kv_norm, fgate_b, lams):
    v = np.zeros((P, NCOL), np.float32)

    def put(name, a):
        v[:a.shape[0], COL[name]:COL[name] + a.shape[1]] = a

    put("gain", np.concatenate([g.reshape(DC, P).T for g in gains], axis=1))
    put("conv_w", conv_w.T.reshape(4, P, TAPS).transpose(1, 0, 2).reshape(P, 4 * TAPS))
    for name, a in (("conv_b", conv_b), ("ln_g", ln_g), ("ln_b", ln_b)):
        put(name, a.reshape(4, P).T)
    for layer, name in enumerate(("ffn2", "ffn3")):
        both = np.concatenate([ffn_w[layer], ffn_b[layer][None]], axis=0)
        put(name, both.reshape(4, 2, FC, P).transpose(3, 2, 1, 0).reshape(P, FC * 8))
    put("subln", subln.reshape(P, 1))
    put("kv_norm", kv_norm.reshape(P, 1))
    put("fgate_b", fgate_b.reshape(HEADS, 1))
    put("lam", np.stack(lams, axis=1))
    row = np.arange(P) % HD
    inv = (np.float32(500000.0) ** (-np.arange(0, 16, 2, dtype=np.float32) / np.float32(16))).astype(np.float32)
    put("freq", np.where(row < 16, inv[row % 8], 0).astype(np.float32)[:, None])
    put("rope_rows", (row < 16).astype(np.float32)[:, None])
    for name, value in (("half_pi", math.pi / 2), ("eps", EPS), ("ln_eps", LN_EPS), ("one", 1.0)):
        v[:, COL[name]] = value
    return v


def kernel(**inputs):
    import concourse.bacc as bacc
    from concourse.bass_utils import run_bass_kernel_spmd

    a = {k: np.asarray(v) for k, v in inputs.items()}
    nc = bacc.Bacc("TRN2", target_bir_lowering=False, num_devices=1)
    bias_rows = np.concatenate([a["rel_bias"], np.full((1, HEADS), NEG, np.float32)], axis=0)
    uk = a["od_w_uk_2"][0].transpose(1, 2, 0)
    uk = np.concatenate([np.zeros((HEADS, 16, RANK), np.float32), uk], axis=1)
    selectors = np.repeat(np.eye(HEADS, dtype=np.float32), P, axis=1)
    arrays = {
        "weights": pack_weights(a["w_in"][0], a["w_out"][0], a["w_gate"][0], a["w_up"][0], a["w_down"][0],
                                a["ev_w_in_2"][0], a["ev_w_out_2"][0], a["od_w_in_2"][0], a["od_w_out_2"][0],
                                a["ffn_w_in_2"], a["ffn_w_out_2"]),
        "vectors": pack_vectors(
            [a["mix_norm_g"][0], a["ffn_norm_g"][0], a["final_norm_g"], a["attn_norm_2"][0],
             a["ffn_norm_2"][0], a["attn_norm_2"][1], a["ffn_norm_2"][1], a["final_norm_2"]],
            a["conv_w"][0], a["conv_b"][0], a["conv_ln_g"][0], a["conv_ln_b"][0],
            a["ffn_conv_w_2"], a["ffn_conv_b_2"], a["ev_subln_2"][0], a["od_kv_norm_2"][0],
            a["ev_fgate_b_2"][0],
            [a["ev_lambda_q1_2"][0], a["ev_lambda_q2_2"][0], a["ev_lambda_k1_2"][0], a["ev_lambda_k2_2"][0]]),
        "x_in": a["x"][0].T.reshape(DC, P, S),
        "positions": a["positions_2"],
        "bias_rows": bias_rows,
        "buckets": bucket_rows(),
        "selectors": selectors,
        "uk": uk.reshape(4, P, RANK).transpose(1, 0, 2),
        "uv": a["od_w_uv_2"][0].reshape(RANK, 512),
        "squares": square_tables(),
    }
    arrays = {k + "_dram": np.ascontiguousarray(v) for k, v in arrays.items()}
    args = [nc.dram_tensor(k, v.shape, mybir.dt.from_np(v.dtype), kind="ExternalInput").ap()
            for k, v in arrays.items()]
    out = nc.dram_tensor("out_dram", (DC, P, S), F32, kind="ExternalOutput").ap()
    build(nc, *args, out)
    r = run_bass_kernel_spmd(nc, [arrays], core_ids=[0])
    return r.results[0]["out_dram"].reshape(D, S).T.reshape(1, S, D)
```
